# Optimizing a Trainium2 kernel written in Bass

```python
import jax, jax.numpy as jnp
from jax import lax
import numpy as np

D_MODEL = 2048
BATCH = 1
SEQ = 512
DEPTH = 1

CONV_GROUPS = 8
CONV_WIDTH = D_MODEL // 2
CONV_K = 3
SGU_GROUPS = 8
SGU_WIDTH = D_MODEL // 2
SGU_GROUP_DIM = SGU_WIDTH // SGU_GROUPS
CHUNK = 128
N_BRANCH = 2
BRANCH_WIDTH = CONV_WIDTH
D_IN = 3 * CONV_WIDTH + 2 * SGU_WIDTH + N_BRANCH * D_MODEL
N_EXPERT_GROUPS = 4
EXPERTS_PER_GROUP = 8
N_EXPERTS = N_EXPERT_GROUPS * EXPERTS_PER_GROUP
TOP_K = 2
D_EXPERT = D_MODEL // 4
MOE_BLOCK = 128
EPS = 1e-6

kernel_name = "hybrid_conv_sgu_hmoe_block"

def rmsnorm(x, g):
    xf = x.astype(jnp.float32)
    y = xf * lax.rsqrt(jnp.mean(xf * xf, axis=-1, keepdims=True) + EPS)
    return (y * g.astype(jnp.float32)).astype(x.dtype)

def layernorm(x, g, b):
    xf = x.astype(jnp.float32)
    mu = jnp.mean(xf, axis=-1, keepdims=True)
    xc = xf - mu
    var = jnp.mean(xc * xc, axis=-1, keepdims=True)
    y = xc * lax.rsqrt(var + EPS)
    return (y * g.astype(jnp.float32) + b.astype(jnp.float32)).astype(x.dtype)

def hybrid_mixer(xn, w_in, b_gate, conv_w, ln_v_g, ln_v_b, sgu_w, sgu_b, w_branch, w_out):
    bsz, s, _ = xn.shape
    proj = xn @ w_in
    c_pre, b_post, xa, z, gates = jnp.split(
        proj, [CONV_WIDTH, 2 * CONV_WIDTH, 3 * CONV_WIDTH, 3 * CONV_WIDTH + 2 * SGU_WIDTH], axis=-1)

    xc = c_pre * xa
    xp = jnp.pad(xc, ((0, 0), (CONV_K - 1, 0), (0, 0)))
    conv = conv_w[0] * xp[:, 0:s]
    for k in range(1, CONV_K):
        conv = conv + conv_w[k] * xp[:, k:k + s]
    y_a = b_post * conv

    z = jax.nn.gelu(z)
    u, v = jnp.split(z, 2, axis=-1)
    v = layernorm(v, ln_v_g, ln_v_b)
    v = v.reshape(bsz, s // CHUNK, CHUNK, SGU_GROUPS, SGU_GROUP_DIM)
    causal = jnp.tril(jnp.ones((CHUNK, CHUNK), dtype=bool))
    ws = jnp.where(causal[None], sgu_w, jnp.zeros_like(sgu_w))
    mixed = jnp.einsum('gts,bnsgc->bntgc', ws, v) + sgu_b.T[:, :, None]
    y_b = u * mixed.reshape(bsz, s, SGU_WIDTH)

    branches = jnp.stack([y_a, y_b], axis=2)
    br = jnp.einsum('bsrw,rwd->bsrd', branches, w_branch)
    g = jax.nn.sigmoid(gates + b_gate).reshape(bsz, s, N_BRANCH, D_MODEL)
    merged = jnp.sum(g * br, axis=2)
    return merged @ w_out

def hier_moe(xn, router_g, router_g_b, router_e, router_e_b, w_gate, w_up, w_down):
    bsz, s, d = xn.shape
    n = bsz * s
    xt = xn.reshape(n, d)
    g_logits = (xt @ router_g + router_g_b).astype(jnp.float32)
    g_prob = jax.nn.softmax(g_logits, axis=-1)
    g_idx = jnp.argmax(g_logits, axis=-1)
    g_w = jnp.take_along_axis(g_prob, g_idx[:, None], axis=1)[:, 0]
    e_logits = (xt @ router_e + router_e_b).astype(jnp.float32).reshape(n, N_EXPERT_GROUPS, EXPERTS_PER_GROUP)
    e_sel = jnp.take_along_axis(e_logits, g_idx[:, None, None], axis=1)[:, 0]
    e_prob = jax.nn.softmax(e_sel, axis=-1)
    top_w, top_i = lax.top_k(e_prob, TOP_K)
    top_w = top_w / jnp.sum(top_w, axis=-1, keepdims=True)
    expert_id = (g_idx[:, None] * EXPERTS_PER_GROUP + top_i).astype(jnp.int32)
    weight = (g_w[:, None] * top_w).astype(xt.dtype)

    a = n * TOP_K
    flat_e = expert_id.reshape(a)
    flat_tok = jnp.repeat(jnp.arange(n, dtype=jnp.int32), TOP_K)
    flat_w = weight.reshape(a)
    order = jnp.argsort(flat_e)
    sorted_e = flat_e[order]
    counts = jnp.bincount(flat_e, length=N_EXPERTS).astype(jnp.int32)
    start = jnp.cumsum(counts) - counts
    padded = (counts + MOE_BLOCK - 1) // MOE_BLOCK * MOE_BLOCK
    pad_end = jnp.cumsum(padded)
    pad_start = pad_end - padded
    rank = jnp.arange(a, dtype=jnp.int32) - start[sorted_e]
    dest = pad_start[sorted_e] + rank
    p = -(-a // MOE_BLOCK) * MOE_BLOCK + N_EXPERTS * MOE_BLOCK
    buf_tok = jnp.zeros((p,), jnp.int32).at[dest].set(flat_tok[order])
    buf_w = jnp.zeros((p,), xt.dtype).at[dest].set(flat_w[order])
    n_blocks = p // MOE_BLOCK
    block_e = jnp.minimum(
        jnp.searchsorted(pad_end, jnp.arange(n_blocks, dtype=jnp.int32) * MOE_BLOCK, side='right'),
        N_EXPERTS - 1)
    xb = xt[buf_tok].reshape(n_blocks, MOE_BLOCK, d)

    def expert_block(args):
        xblk, e = args
        h = jax.nn.silu(xblk @ w_gate[e]) * (xblk @ w_up[e])
        return h @ w_down[e]

    yb = lax.map(expert_block, (xb, block_e))
    y = jax.ops.segment_sum(yb.reshape(p, d) * buf_w[:, None], buf_tok, num_segments=n)
    return y.reshape(bsz, s, d)

def setup_inputs(seed: int = 0) -> dict:
    key = jax.random.key(seed)
    ks = jax.random.split(key, 24)

    def nrm(k, shape, scale):
        return jax.random.normal(k, shape, jnp.float32) * scale

    d = D_MODEL
    return {
        "x": nrm(ks[0], (BATCH, SEQ, d), 1.0),
        "norm1_g": 1.0 + nrm(ks[1], (DEPTH, d), 0.02),
        "w_in": nrm(ks[2], (DEPTH, d, D_IN), d ** -0.5),
        "b_gate": nrm(ks[3], (DEPTH, N_BRANCH * d), 0.02),
        "conv_w": nrm(ks[4], (DEPTH, CONV_K, CONV_WIDTH), CONV_K ** -0.5),
        "ln_v_g": 1.0 + nrm(ks[5], (DEPTH, SGU_WIDTH), 0.02),
        "ln_v_b": nrm(ks[6], (DEPTH, SGU_WIDTH), 0.02),
        "sgu_w": nrm(ks[7], (DEPTH, SGU_GROUPS, CHUNK, CHUNK), CHUNK ** -0.5),
        "sgu_b": 1.0 + nrm(ks[8], (DEPTH, SGU_GROUPS, CHUNK), 0.02),
        "w_branch": nrm(ks[9], (DEPTH, N_BRANCH, BRANCH_WIDTH, d), BRANCH_WIDTH ** -0.5),
        "w_out": nrm(ks[10], (DEPTH, d, d), d ** -0.5),
        "norm2_g": 1.0 + nrm(ks[11], (DEPTH, d), 0.02),
        "router_g": nrm(ks[12], (DEPTH, d, N_EXPERT_GROUPS), d ** -0.5),
        "router_g_b": nrm(ks[13], (DEPTH, N_EXPERT_GROUPS), 0.01),
        "router_e": nrm(ks[14], (DEPTH, d, N_EXPERTS), d ** -0.5),
        "router_e_b": nrm(ks[15], (DEPTH, N_EXPERTS), 0.01),
        "w_gate": nrm(ks[16], (DEPTH, N_EXPERTS, d, D_EXPERT), d ** -0.5),
        "w_up": nrm(ks[17], (DEPTH, N_EXPERTS, d, D_EXPERT), d ** -0.5),
        "w_down": nrm(ks[18], (DEPTH, N_EXPERTS, D_EXPERT, d), D_EXPERT ** -0.5),
        "final_g": 1.0 + nrm(ks[19], (d,), 0.02),
    }

def reference(x, norm1_g, w_in, b_gate, conv_w, ln_v_g, ln_v_b, sgu_w, sgu_b, w_branch, w_out,
              norm2_g, router_g, router_g_b, router_e, router_e_b, w_gate, w_up, w_down, final_g):
    h = x
    for l in range(DEPTH):
        h = h + hybrid_mixer(rmsnorm(h, norm1_g[l]), w_in[l], b_gate[l], conv_w[l], ln_v_g[l], ln_v_b[l],
                             sgu_w[l], sgu_b[l], w_branch[l], w_out[l])
        h = h + hier_moe(rmsnorm(h, norm2_g[l]), router_g[l], router_g_b[l], router_e[l], router_e_b[l],
                         w_gate[l], w_up[l], w_down[l])
    return rmsnorm(h, final_g)


_drawn_inputs = setup_inputs


def setup_inputs(seed=0):
    import zlib

    import numpy as np

    out = dict(_drawn_inputs(seed))
    spreads = {}
    factors = {'b_gate': 3.573,
     'ln_v_g': 18.981,
     'ln_v_b': 21.524,
     'sgu_b': 14.431,
     'router_g_b': 17.749,
     'router_e_b': 22.021,
     'final_g': 8.479,
     'norm2_g': 4.738}
    for name, (base, spread) in spreads.items():
        noise = np.random.default_rng([zlib.crc32(name.encode()), seed]).standard_normal(out[name].shape)
        drawn = base * np.exp(spread * noise) if base else spread * noise
        out[name] = __import__('jax').numpy.asarray(drawn.astype(out[name].dtype))
    for name, factor in factors.items():
        out[name] = (out[name] * factor).astype(out[name].dtype)
    return out
```

```python
from contextlib import ExitStack

import concourse.bass as bass
from concourse import mybir

P = 128
F32 = mybir.dt.float32
F32R = mybir.dt.float32r
BF16 = mybir.dt.bfloat16
I32 = mybir.dt.int32
ALU = mybir.AluOpType
ACT = mybir.ActivationFunctionType
AX = mybir.AxisListType.X

EPS = 1e-6
CB = 512
CK = 2
RAW_SLOTS = 4
SPLIT_SLOTS = 2
EK = 4
CAP = 64
MAX_OVER = 16
RING = 8


def hybrid_block(nc, x, norm1_g, mixer_w, b_gate, conv_w, ln_v_g, ln_v_b, sgu_w, sgu_b,
                 norm2_g, router_w, router_b, expert_w, final_g, consts, out):
    _, N, D = x.shape
    W = ln_v_g.shape[1]
    G = sgu_w.shape[1]
    KT, NT, WT = D // P, N // P, W // P
    KC, WC = KT // CK, WT // CK
    DB, WB = D // CB, W // CB
    MB = CB // P
    assert NT == 4 and MB == 4 and sgu_w.shape[2] == P

    EG = 4
    E = router_w.shape[2] - EG
    EPG = E // EG
    PAIRS = E // 2
    assert CAP + (P // E) * 2 * CAP >= N and 2 * N // (CAP + 1) < MAX_OVER
    KX = D // (EK * P)
    DX = D // CB
    LX = 2 * KX + DX
    USED = LX
    assert 2 * LX % RING == 0 and EK * P == CB and MB == EK

    x_v = x[0].rearrange("(m p) d -> p m d", p=P)
    out_v = out[0].rearrange("(m p) d -> p m d", p=P)

    Q_V = 0
    Q_CONV = Q_V + WB * KC
    Q_U = Q_CONV + WB * 3 * KC
    Q_MERGE = Q_U + WB * KC
    Q_OUT = Q_MERGE + DB * 2 * (KC + WC)
    Q_END = Q_OUT + DB * KC

    with ExitStack() as ctx:
        def sb(name, shape, dt=F32):
            return ctx.enter_context(nc.sbuf_tensor(name, shape, dt))

        def sem(name):
            return ctx.enter_context(nc.semaphore(name))

        const = sb("const", [P, consts.shape[1]])
        ident, wide = const[:, 0:P], const[:, P:5 * P]
        iota_c = const[:, 5 * P:5 * P + CAP]
        iota_u = const[:, 5 * P + CAP:5 * P + CAP + MAX_OVER]
        desc_g = const[:, 5 * P + CAP + MAX_OVER:5 * P + CAP + MAX_OVER + EG]
        desc_e = const[:, 5 * P + CAP + MAX_OVER + EG:5 * P + CAP + MAX_OVER + EG + EPG]
        constb = sb("constb", [P, 4, P], BF16)
        before, ones, cand_e, cand_r = (constb[:, k] for k in range(4))
        pos = sb("pos", [P, NT, E])
        w32 = sb("w32", [P, NT, E])
        pc, wc = sb("pc", [P, NT, 2]), sb("wc", [P, NT, 2])
        wsl = sb("wsl", [P, 1])
        over_n, over_e = sb("over_n", [1, 1], I32), sb("over_e", [1, MAX_OVER], I32)
        over_r = sb("over_r", [P, MAX_OVER])
        bgate = sb("bgate", [P, 2 * KT])
        convw = sb("convw", [P, 3, WT])
        sumsq = sb("sumsq", [P, NT])
        rstd = sb("rstd", [P, NT])
        var = sb("var", [P, NT])
        rvar = sb("rvar", [P, NT])
        bnst = sb("bnst", [P, NT, 2, 6])
        bnag = sb("bnag", [P, NT, 2])

        BASE = 24544
        assert nc.sbuf_base <= BASE, nc.sbuf_base

        def at(name, shape, dt, kib):
            return nc.alloc_sbuf_tensor_at(name, shape, dt, offset=BASE + int(kib * 1024))

        xh, xl = at("xh", [P, KT, N], F32R, 0), at("xl", [P, KT, N], F32R, 32)
        mh, ml = at("mh", [P, KT, N], F32R, 0), at("ml", [P, KT, N], F32R, 32)
        yah, yal = at("yah", [P, WT, N], F32R, 64), at("yal", [P, WT, N], F32R, 80)
        ybh, ybl = at("ybh", [P, WT, N], F32R, 96), at("ybl", [P, WT, N], F32R, 112)
        xnat = at("xnat", [P, NT, D], F32, 64)
        g1bc = at("g1bc", [P, D], F32, 96)
        wsraw = at("wsraw", [P, G, P], F32, 104)
        cbuf = at("cbuf", [P, MB, N], F32, 96)
        xc = at("xc", [P, MB, N + 2], F32, 104)
        lng, lnb = at("lng", [P, W], F32, 116), at("lnb", [P, W], F32, 120)
        h = at("h", [P, NT, D], F32, 64)
        v = at("v", [P, NT, W], F32, 128)
        wst = at("wst", [P, G, P], F32, 144)
        sgub = at("sgub", [P, G, P], F32, 148)
        mx = at("mx", [P, MB, N], F32, 152)
        mrg = at("mrg", [P, KT, N], F32, 128)
        raw = at("raw", [P, RAW_SLOTS, CK, CB], F32, 160)
        wh = at("wh", [P, SPLIT_SLOTS, CK, CB], F32R, 176)
        wl = at("wl", [P, SPLIT_SLOTS, CK, CB], F32R, 184)
        sg = at("sg", [P, MB, N], F32, 192)

        ring = [at(f"ring{s}", [P, EK, CB], F32, 96 + 8 * s) for s in range(RING)]
        xn = at("xn", [P, NT, D], F32, 160)
        g2bc = at("g2bc", [P, D], F32, 56)
        xb = at("xb", [P, 3, NT, D], BF16, 0)
        xt = at("xt", [P, 2, KT, P], F32, 48)
        xg = at("xg", [P, KT, P], F32, 48)
        hh, sl = at("hh", [P, CB], F32, 56), at("sl", [P, CB], F32, 58)
        ht = at("ht", [P, EK, P], F32, 60)
        selb = at("selb", [P, NT, P], BF16, 62)
        self_ = at("self_", [P, NT, P], F32, 160)
        selt = at("selt", [P, NT, P], F32R, 162)
        yh, yl = at("yh", [P, 2, CB], F32R, 164), at("yl", [P, 2, CB], F32R, 168)
        fgbc = at("fgbc", [P, D], F32, 176)
        place = [192 * 1024]

        def rt(name, shape, dt=F32):
            t = nc.alloc_sbuf_tensor_at(name, shape, dt, offset=BASE + place[0])
            n = 4 if dt == F32 else 2
            for k in shape[1:]:
                n *= k
            place[0] += (n + 31) // 32 * 32
            assert place[0] <= 200 * 1024 - 64
            return t

        rw = rt("rw", [P, KT, EG + E])
        rb = rt("rb", [P, EG + E])
        lg = rt("lg", [P, NT, EG + E])
        gmax, gsum, gw, gtop = (rt(n, [P, NT, 1]) for n in ("gmax", "gsum", "gw", "gtop"))
        gsh, gexp, gcode, goh = (rt(n, [P, NT, EG]) for n in ("gsh", "gexp", "gcode", "goh"))
        emask = rt("emask", [P, NT, EG, EPG])
        esel, esh, eexp, ecode, oh1, es2, oh2, m8, p8 = (
            rt(n, [P, NT, EPG]) for n in ("esel", "esh", "eexp", "ecode", "oh1", "es2", "oh2", "m8", "p8"))
        emax, etop, den, rden = (rt(n, [P, NT, 1]) for n in ("emax", "etop", "den", "rden"))
        m32 = rt("m32", [P, NT, EG, EPG])
        m32b = rt("m32b", [P, NT, E], BF16)
        msum = rt("msum", [P, E])
        m128 = rt("m128", [P, E, P // E], BF16)
        active = rt("active", [P, 1])
        activeb = rt("activeb", [P, 1], BF16)
        prefix = rt("prefix", [P, 1])
        unit_oh = rt("unit_oh", [P, MAX_OVER])
        unit_ohb = rt("unit_ohb", [P, MAX_OVER], BF16)
        over_nf = rt("over_nf", [P, 1])

        ps = ctx.enter_context(nc.psum_tensor("ps", [P, 8, CB], F32))

        x_in = [sem(f"x_in{m}") for m in range(NT)]
        g1_in = sem("g1_in")
        ws_in = sem("ws_in")
        small_in = sem("small_in")
        h_in = sem("h_in")
        raw_in = [sem(f"raw_in{s}") for s in range(RAW_SLOTS)]
        const_in, router_in, constb_ready = sem("const_in"), sem("router_in"), sem("constb_ready")
        sq_done, rvar_ready, root_done, xn_ready = sem("sq_done"), sem("rvar_ready"), sem("root_done"), sem("xn_ready")
        tr_done, tr_hi, tr_lo = sem("tr_done"), sem("tr_hi"), sem("tr_lo")
        ws_masked, wst_tr, wst_ready = sem("ws_masked"), sem("wst_tr"), sem("wst_ready")
        hi_done, lo_done, pe_chunk = sem("hi_done"), sem("lo_done"), sem("pe_chunk")
        set_free = [sem("set_free0"), sem("set_free1")]
        v_gelu, v_ready = sem("v_gelu"), sem("v_ready")
        pad_zero = sem("pad_zero")
        ya_ready, yb_ready = sem("ya_ready"), sem("yb_ready")
        mixed_done, u_ready, u_used = sem("mixed_done"), sem("u_ready"), sem("u_used")
        sg_ready, mrg_sum = sem("sg_ready"), sem("mrg_sum")
        m_ready, h_ready = sem("m_ready"), [sem("h_ready0"), sem("h_ready1")]
        g2_in, fg_in = sem("g2_in"), sem("fg_in")
        xn2_ready, xb0_ready, xt_done, xt_ready, xb1_ready, xr_done = (
            sem(n) for n in ("xn2_ready", "xb0_ready", "xt_done", "xt_ready", "xb1_ready", "xr_done"))
        logit_done, gsh_ready, gexp_ready, esh_ready, eexp_ready = (
            sem(n) for n in ("logit_done", "gsh_ready", "gexp_ready", "esh_ready", "eexp_ready"))
        mask_ready, rank_done, active_ready, prefix_done, unit_ready, table_done, table_ready = (
            sem(n) for n in ("mask_ready", "rank_done", "active_ready", "prefix_done", "unit_ready", "table_done",
                             "table_ready"))
        ring_in = [sem(f"ring_in{s}") for s in range(RING)]
        sel_ready, gat_done, xg_done, seltr_done, selt_done = (
            sem(n) for n in ("sel_ready", "gat_done", "xg_done", "seltr_done", "selt_done"))
        used, silu_done, h_done, htr_done, ht_ready = (
            sem(n) for n in ("used", "silu_done", "h_done", "htr_done", "ht_ready"))
        yh_done, y_split, cb_done, add_done, moe_done = (
            sem(n) for n in ("yh_done", "y_split", "cb_done", "add_done", "moe_done"))
        out_ready = sem("out_ready")
        dve_step = sem("dve_step")
        stored = sem("stored")

        CREDITS = ((set_free[0], 1), (set_free[1], 1), (u_used, 1), (mrg_sum, 1), (sg_ready, 1), (h_ready[0], 1),
                   (h_ready[1], 1), (xg_done, 2), (y_split, 2), (add_done, 2), (cb_done, 5), (h_done, 1))

        block = ctx.enter_context(nc.Block())

        N_SMALL = 5

        @block.sync
        def _(sp):
            for m in range(NT):
                sp.dma_start(xnat[:, m], x_v[:, m]).then_inc(x_in[m], 16)
                if m == 0:
                    sp.dma_start(g1bc[:], norm1_g.partition_broadcast(P).rearrange("p o d -> p (o d)")).then_inc(g1_in, 16)

            def chunk(q, s):
                sp.dma_start(raw[:, s], mixer_w[bass.ds(q, 1)].rearrange("o p f -> (o p) f")).then_inc(raw_in[s], 16)

            for s in range(RAW_SLOTS):
                chunk(s, s)
            with sp.Fori(1, Q_OUT // RAW_SLOTS) as i:
                for s in range(RAW_SLOTS):
                    sp.wait_ge(lo_done, i * RAW_SLOTS + (s - RAW_SLOTS + 1))
                    chunk(i * RAW_SLOTS + s, s)
            sp.wait_ge(pe_chunk, Q_OUT)
            sp.dma_start(h[:], x_v).then_inc(h_in, 16)

            def out_chunks(i):
                for s in range(RAW_SLOTS):
                    sp.wait_ge(lo_done, i * RAW_SLOTS + (s - RAW_SLOTS + 1))
                    chunk(i * RAW_SLOTS + s, s)

            def expert_chunk(q, s):
                sp.dma_start(ring[s][:].rearrange("p j n -> p (j n)"),
                             expert_w[bass.ds(q, 1)].rearrange("o p f -> (o p) f")).then_inc(ring_in[s], 16)

            lead, tail = Q_OUT // RAW_SLOTS + 2, Q_END // RAW_SLOTS - 2
            with sp.Fori(Q_OUT // RAW_SLOTS, lead) as i:
                out_chunks(i)
            sp.wait_ge(m_ready, KT)
            for i in range(lead, tail):
                out_chunks(i)
                for c in (2 * (i - lead), 2 * (i - lead) + 1):
                    expert_chunk((c % 2) * LX + c // 2, c)
            with sp.Fori(tail, Q_END // RAW_SLOTS) as i:
                out_chunks(i)
            sp.wait_ge(pe_chunk, Q_END)
            sp.dma_start(g2bc[:], norm2_g.partition_broadcast(P).rearrange("p o d -> p (o d)")).then_inc(g2_in, 16)

            def unit_chunks(u, first, last, expert):
                for c in range(first, last):
                    sp.wait_ge(used, u * USED + (c // 2 - RING // 2 + 1))
                    expert_chunk(expert(c % 2) * LX + c // 2, c % RING)

            with sp.Fori(0, PAIRS - 1) as u:
                unit_chunks(u, RING, 2 * LX, lambda ab: u * 2 + ab)
                unit_chunks(u + 1, 0, RING, lambda ab: u * 2 + (2 + ab))
            for c in range(RING, 2 * LX):
                sp.wait_ge(used, (PAIRS - 1) * USED + c // 2 - RING // 2 + 1)
                expert_chunk((E - 2 + c % 2) * LX + c // 2, c % RING)
            sp.wait_ge(sel_ready, 1)
            sp.dma_start(fgbc[:], final_g.partition_broadcast(P).rearrange("p o d -> p (o d)")).then_inc(fg_in, 16)
            sp.wait_ge(table_ready, 1)
            n_over = sp.value_load(over_n[0:1, 0:1], min_val=0, max_val=MAX_OVER - 1)
            with sp.Fori(0, MAX_OVER - 1) as i:
                with sp.If(i < n_over):
                    e = sp.value_load(over_e[0:1, bass.ds(i, 1)], min_val=0, max_val=E - 1)
                    unit_chunks(i + PAIRS, 0, 2 * LX, lambda ab: e)
            for m in range(NT):
                sp.wait_ge(out_ready, m + 1)
                sp.dma_start(out_v[:, m], h[:, m]).then_inc(stored, 16)
            sp.wait_ge(stored, 16 * NT)

        @block.gpsimd
        def _(pool):
            pool.wait_ge(ws_in, 16)
            nc.gpsimd.affine_select(out=wsraw[:], in_=wsraw[:], compare_op=ALU.is_ge, fill=0.0, base=0,
                                    pattern=[[0, G], [-1, P]], channel_multiplier=1).then_inc(ws_masked, 1)

            with pool.Fori(0, Q_END // RAW_SLOTS) as i:
                for c in range(RAW_SLOTS):
                    pool.wait_ge(hi_done, i * RAW_SLOTS + c + 1)
                    s = c % SPLIT_SLOTS
                    nc.gpsimd.tensor_tensor(wl[:, s], raw[:, c], wh[:, s].bitcast(F32), ALU.subtract).then_inc(lo_done, 1)

            for m in range(NT):
                pool.wait_ge(xn2_ready, m + 1)
                nc.gpsimd.tensor_copy(xb[:, 0, m], xn[:, m]).then_inc(xb0_ready, 1)

        @block.scalar
        def _(act):
            act.dma_start(const[:], consts).then_inc(const_in, 16)
            act.dma_start(wsraw[:], sgu_w[0].rearrange("g t s -> t g s")).then_inc(ws_in, 16)
            act.dma_start(bgate[:], b_gate).then_inc(small_in, 16)
            act.dma_start(convw[:], conv_w).then_inc(small_in, 16)
            act.dma_start(lng[:], ln_v_g.partition_broadcast(P).rearrange("p o d -> p (o d)")).then_inc(small_in, 16)
            act.dma_start(lnb[:], ln_v_b.partition_broadcast(P).rearrange("p o d -> p (o d)")).then_inc(small_in, 16)
            act.dma_start(sgub[:], sgu_b.partition_broadcast(P).rearrange("p o g t -> p (o g) t")).then_inc(small_in, 16)

            def root(n):
                act.wait_ge(rvar_ready, n)
                nc.scalar.activation(rstd[:], rvar[:], ACT.Sqrt).then_inc(root_done, 1)

            for m in range(NT):
                act.wait_ge(x_in[m], 16)
                if m >= 1:
                    act.wait_ge(sq_done, m)
                nc.scalar.activation(ps[:, 0:4].rearrange("p a b -> p (a b)"), xnat[:, m], ACT.Square,
                                     accum_out=sumsq[:, m:m + 1]).then_inc(sq_done, 1)
            root(1)
            for t in range(NT * KT // 4):
                m, kc = t // (KT // 4), t % (KT // 4)
                act.wait_ge(tr_done, t + 1)
                nc.scalar.activation(xh[:, 4 * kc:4 * kc + 4, m * P:(m + 1) * P],
                                     ps[:, 4 + t % 4].rearrange("p (k n) -> p k n", k=4), ACT.Copy).then_inc(tr_hi, 1)

            def hi(q, c):
                if isinstance(q, int):
                    use = (q + c) // RAW_SLOTS + 1
                else:
                    use = q // RAW_SLOTS + c // RAW_SLOTS + 1
                act.wait_ge(raw_in[c % RAW_SLOTS], use * 16)
                if not isinstance(q, int) or q + c >= SPLIT_SLOTS:
                    act.wait_ge(pe_chunk, q + c - SPLIT_SLOTS + 1)
                nc.scalar.activation(wh[:, c % SPLIT_SLOTS], raw[:, c % RAW_SLOTS], ACT.Copy).then_inc(hi_done, 1)

            def hi_at(i, q0, per, c):
                act.wait_ge(raw_in[c % RAW_SLOTS], i * (16 * per // RAW_SLOTS) + 16 * ((q0 + c) // RAW_SLOTS + 1))
                act.wait_ge(pe_chunk, i * per + (q0 + c - SPLIT_SLOTS + 1))
                nc.scalar.activation(wh[:, c % SPLIT_SLOTS], raw[:, c % RAW_SLOTS], ACT.Copy).then_inc(hi_done, 1)

            hi(0, 0)
            hi(0, 1)
            for i in range(WB):
                for c in range(KC):
                    hi(Q_V + i * KC, 2 + c)
                for m in range(MB):
                    act.wait_ge(pe_chunk, Q_V + (i + 1) * KC)
                    nc.scalar.activation(v[:, m, i * CB:(i + 1) * CB], ps[:, 4 * i + m], ACT.Gelu_apprx_tanh
                                         ).then_inc(v_gelu, 1)
            root(2)
            with act.Fori(0, WB) as i:
                for c in range(3 * KC):
                    hi_at(i, Q_CONV, 3 * KC, 2 + c)
            with act.Fori(0, WB) as i:
                for c in range(KC):
                    hi_at(i, Q_U, KC, 2 + c)
                act.wait_ge(pe_chunk, i * KC + Q_U + KC)
                act.wait_ge(u_used, i + 1)
                for m in range(MB):
                    nc.scalar.activation(sg[:, m], ps[:, m], ACT.Gelu_apprx_tanh).then_inc(u_ready, 1)
            with act.Fori(0, DB) as i:
                for r in range(2):
                    q = r * (KC + WC)
                    for c in range(KC):
                        hi_at(i, Q_MERGE, 2 * (KC + WC), q + 2 + c)
                    act.wait_ge(pe_chunk, i * 2 * (KC + WC) + (Q_MERGE + q + KC))
                    if r == 0:
                        act.wait_ge(u_used, WB + 1)
                        act.wait_ge(mrg_sum, i + 1)
                    else:
                        act.wait_ge(set_free[1], 2 * i + (2 * WB + 2))
                    for m in range(MB):
                        nc.scalar.activation(sg[:, m], ps[:, m], ACT.Sigmoid,
                                             bias=bgate[:, bass.ds(i * MB + r * KT + m, 1)]).then_inc(sg_ready, 1)
                    for c in range(WC):
                        hi_at(i, Q_MERGE, 2 * (KC + WC), q + KC + 2 + c)
            with act.Fori(0, DB - 1) as i:
                for c in range(KC):
                    hi_at(i, Q_OUT, KC, 2 + c)
            for c in range(2, KC):
                hi(Q_OUT + (DB - 1) * KC, c)

            def squares(free, n):
                for m in range(NT):
                    free(m)
                    nc.scalar.activation(ps[:, 0:4].rearrange("p a b -> p (a b)"), h[:, m], ACT.Square,
                                         accum_out=sumsq[:, m:m + 1]).then_inc(sq_done, 1)
                    act.wait_ge(sq_done, n * NT + m + 1)
                root(n + 2)

            def mixer_ready(m):
                act.wait_ge(h_ready[0], NT * DB // 2 + 1)
                act.wait_ge(h_ready[1], NT * (DB // 2 - 1) + m + 2)

            squares(mixer_ready, 1)
            act.dma_start(rw[:], router_w).then_inc(router_in, 16)
            act.dma_start(rb[:], router_b.partition_broadcast(P).rearrange("p o d -> p (o d)")).then_inc(router_in, 16)
            for m in range(NT):
                for kc in range(KT // 4):
                    t = m * (KT // 4) + kc
                    act.wait_ge(xt_done, t + 1)
                    if m >= 2:
                        act.wait_ge(logit_done, m - 1)
                    nc.scalar.activation(xt[:, m % 2, 4 * kc:4 * kc + 4], ps[:, 4 + t % 4].rearrange("p (k n) -> p k n", k=4),
                                         ACT.Copy).then_inc(xt_ready, 1)
                act.wait_ge(xr_done, 2 * m + 1)
                nc.scalar.activation(xb[:, 1, m], xn[:, m], ACT.Copy).then_inc(xb1_ready, 1)
            act.wait_ge(gsh_ready, 1)
            nc.scalar.activation(gexp[:], gsh[:], ACT.Exp).then_inc(gexp_ready, 1)
            act.wait_ge(esh_ready, 1)
            nc.scalar.activation(eexp[:], esh[:], ACT.Exp).then_inc(eexp_ready, 1)

            def gathered(u):
                for kc in range(KT // 4):
                    act.wait_ge(gat_done, u * (KT // 4) + (kc + 1))
                    nc.scalar.activation(xg[:, 4 * kc:4 * kc + 4], ps[:, 6 + kc % 2].rearrange("p (k n) -> p k n", k=4),
                                         ACT.Copy).then_inc(xg_done, 1)

            def silu(u):
                act.wait_ge(used, u * USED + (2 * KX - 1))
                act.wait_ge(h_done, u + 1)
                nc.scalar.activation(sl[:], ps[:, 0], ACT.Silu).then_inc(silu_done, 1)

            def high_y(u):
                for c in range(DX):
                    act.wait_ge(used, u * USED + (2 * KX + c + 1))
                    act.wait_ge(cb_done, u * 4 * NT + (NT * c - NT + 5 if c else 1))
                    nc.scalar.activation(yh[:, c % 2], ps[:, 2 + c % 2], ACT.Copy).then_inc(yh_done, 1)

            gathered(0)
            with act.Fori(0, PAIRS - 1) as u:
                silu(u)
                act.wait_ge(used, u * USED + 2 * KX)
                gathered(u + 1)
                high_y(u)
            silu(PAIRS - 1)
            high_y(PAIRS - 1)
            act.wait_ge(table_ready, 1)
            n_over = act.value_load(over_n[0:1, 0:1], min_val=0, max_val=MAX_OVER - 1)
            with act.Fori(0, MAX_OVER - 1) as i:
                with act.If(i < n_over):
                    gathered(i + PAIRS)
                    silu(i + PAIRS)
                    high_y(i + PAIRS)
            squares(lambda m: act.wait_ge(moe_done, 1), 2)

        @block.tensor
        def _(pe):
            pe.wait_ge(const_in, 16)
            for t in range(NT * KT // 4):
                m, kc = t // (KT // 4), t % (KT // 4)
                pe.wait_ge(xn_ready, m + 1)
                if t >= 4:
                    pe.wait_ge(tr_lo, t - 3)
                for j in range(4):
                    k = 4 * kc + j
                    last = nc.tensor.transpose(ps[:, 4 + t % 4, j * P:(j + 1) * P], xnat[:, m, k * P:(k + 1) * P], ident)
                last.then_inc(tr_done, 1)
            pe.wait_ge(ws_masked, 1)
            pe.wait_ge(sq_done, NT)
            for g in range(G):
                last = nc.tensor.transpose(ps[:, g // 4, (g % 4) * P:(g % 4 + 1) * P], wsraw[:, g], ident)
            last.then_inc(wst_tr, 1)
            pe.wait_ge(wst_ready, 1)
            pe.wait_ge(tr_lo, NT * KT // 4)

            def channel_block(ah, al, kts, base, q):
                for c in range(kts // CK):
                    pe.wait_ge(lo_done, q + c + 1)
                    for j in range(CK):
                        k = c * CK + j
                        for m in range(MB):
                            o = ps[:, base + m]
                            whi = wh[:, c % SPLIT_SLOTS, j, m * P:(m + 1) * P]
                            wlo = wl[:, c % SPLIT_SLOTS, j, m * P:(m + 1) * P]
                            nc.tensor.matmul(o, whi, ah[:, k], start=(k == 0), stop=False)
                            nc.tensor.matmul(o, whi, al[:, k], start=False, stop=False)
                            last = nc.tensor.matmul(o, wlo, ah[:, k], start=False, stop=(k == kts - 1))
                    last.then_inc(pe_chunk, 1)

            def token_block(ah, al, base, q, ready=None):
                for c in range(KC):
                    pe.wait_ge(lo_done, q + c + 1)
                    for j in range(CK):
                        k = c * CK + j
                        if ready is not None:
                            pe.wait_ge(ready, k + 1)
                        for m in range(NT):
                            o = ps[:, base + m]
                            xhi = ah[:, k, m * P:(m + 1) * P]
                            xlo = al[:, k, m * P:(m + 1) * P]
                            nc.tensor.matmul(o, xhi, wh[:, c % SPLIT_SLOTS, j], start=(k == 0), stop=False)
                            nc.tensor.matmul(o, xhi, wl[:, c % SPLIT_SLOTS, j], start=False, stop=False)
                            last = nc.tensor.matmul(o, xlo, wh[:, c % SPLIT_SLOTS, j], start=False, stop=(k == KT - 1))
                    last.then_inc(pe_chunk, 1)

            for i in range(WB):
                token_block(xh, xl, 4 * i, Q_V + i * KC)
            with pe.Fori(0, WB) as i:
                q = i * 3 * KC + Q_CONV
                pe.wait_ge(v_gelu, MB * WB)
                pe.wait_ge(set_free[0], 2 * i + 1)
                channel_block(xh, xl, KT, 0, q)
                pe.wait_ge(set_free[1], i + 1)
                channel_block(xh, xl, KT, 4, q + KC)
                pe.wait_ge(set_free[0], 2 * i + 2)
                channel_block(xh, xl, KT, 0, q + 2 * KC)
            for i in range(WB):
                pe.wait_ge(v_ready, NT)
                pe.wait_ge(set_free[1], WB + i + 1)
                for m in range(MB):
                    g = i * MB + m
                    for n in range(NT):
                        last = nc.tensor.matmul(ps[:, 4 + m, n * P:(n + 1) * P], v[:, n, g * P:(g + 1) * P],
                                                wst[:, g], start=True, stop=True)
                last.then_inc(mixed_done, 1)
                if i == 0:
                    pe.wait_ge(set_free[0], 2 * WB + 1)
                else:
                    pe.wait_ge(u_ready, MB * i)
                channel_block(xh, xl, KT, 0, Q_U + i * KC)
            with pe.Fori(0, DB) as i:
                for r in range(2):
                    q = i * 2 * (KC + WC) + (Q_MERGE + r * (KC + WC))
                    pe.wait_ge(u_ready, MB * WB)
                    pe.wait_ge(sg_ready, i * 2 * MB + (MB * r + 1))
                    channel_block(xh, xl, KT, 0, q)
                    pe.wait_ge(ya_ready if r == 0 else yb_ready, WB)
                    pe.wait_ge(set_free[1], i * 2 + (2 * WB + r + 1))
                    channel_block(yah if r == 0 else ybh, yal if r == 0 else ybl, WT, 4, q + KC)
            with pe.Fori(0, DB // 2) as i:
                for s in range(2):
                    if s == 0:
                        pe.wait_ge(sg_ready, 2 * MB * DB + 1)
                    else:
                        pe.wait_ge(set_free[1], 2 * WB + 2 * DB + 1)
                    pe.wait_ge(h_ready[s], i * NT + 1)
                    token_block(mh, ml, 4 * s, i * 2 * KC + (Q_OUT + s * KC), ready=m_ready)

            for m in range(NT):
                for kc in range(KT // 4):
                    t = m * (KT // 4) + kc
                    pe.wait_ge(xn2_ready, m + 1)
                    if t >= 4:
                        pe.wait_ge(xt_ready, t - 3)
                    else:
                        pe.wait_ge(h_ready[1], NT * (DB // 2) + 1)
                    for j in range(4):
                        k = 4 * kc + j
                        last = nc.tensor.transpose(ps[:, 4 + t % 4, j * P:(j + 1) * P], xn[:, m, k * P:(k + 1) * P], ident)
                    last.then_inc(xt_done, 1)
                pe.wait_ge(router_in, 32)
                pe.wait_ge(sq_done, 2 * NT)
                for k in range(KT):
                    if k % 4 == 0:
                        pe.wait_ge(xt_ready, m * (KT // 4) + k // 4 + 1)
                    last = nc.tensor.matmul(ps[:, m, 0:EG + E], xt[:, m % 2, k], rw[:, k], start=(k == 0), stop=(k == KT - 1))
                last.then_inc(logit_done, 1)

            pe.wait_ge(constb_ready, 1)
            pe.wait_ge(mask_ready, 1)
            pe.wait_ge(xt_ready, NT * KT // 4)
            for n in range(NT):
                for b in range(n + 1):
                    nc.tensor.matmul(ps[:, 4, n * E:(n + 1) * E], before if b == n else ones, m32b[:, b],
                                     start=(b == 0), stop=(b == n))
            nc.tensor.matmul(ps[:, 5, 0:1], m128[:].rearrange("p e t -> p (e t)"), ones[:, 0:1], start=True, stop=True
                             ).then_inc(rank_done, 1)
            pe.wait_ge(active_ready, 1)
            nc.tensor.matmul(ps[:, 5, 2:3], before, activeb[:], start=True, stop=True).then_inc(prefix_done, 1)
            pe.wait_ge(unit_ready, 1)
            for k, t in enumerate((cand_e, cand_r, ones)):
                last = nc.tensor.matmul(ps[:, 6, k * MAX_OVER:(k + 1) * MAX_OVER], t, unit_ohb[:], start=True, stop=True)
            last.then_inc(table_done, 1)

            HALF = (slice(0, CAP), slice(CAP, 2 * CAP))

            def gather(u):
                pe.wait_ge(sel_ready, u + 1)
                for kc in range(KT // 4):
                    pe.wait_ge(xg_done, u * (KT // 4) + (kc + 1))
                    for j in range(4):
                        k = 4 * kc + j
                        for n in range(NT):
                            for b in range(3):
                                last = nc.tensor.matmul(ps[:, 6 + kc % 2, j * P:(j + 1) * P], xb[:, b, n, k * P:(k + 1) * P],
                                                        selb[:, n], start=(n == 0 and b == 0), stop=(n == NT - 1 and b == 2))
                    last.then_inc(gat_done, 1)

            def turn_selection(u):
                pe.wait_ge(xg_done, (u + 1) * (KT // 4) + 2)
                for n in range(NT):
                    nc.tensor.transpose(ps[:, 6, n * P:(n + 1) * P], self_[:, n], ident)
                for n in range(NT):
                    last = nc.tensor.matmul(ps[:, 7, 0:2], self_[:, n], wc[:, n], start=(n == 0), stop=(n == NT - 1))
                last.then_inc(seltr_done, 1)

            def landed(u, c):
                pe.wait_ge(ring_in[c % RING], u * (2 * LX // RING * 16) + (c // RING + 1) * 16)

            def gate_up(u):
                for l in range(2 * KX):
                    landed(u, 2 * l)
                    landed(u, 2 * l + 1)
                    kc = l // 2
                    for j in range(EK):
                        for ab in range(2):
                            last = nc.tensor.matmul(ps[HALF[ab], l % 2], xg[:, EK * kc + j, HALF[ab]],
                                                    ring[(2 * l + ab) % RING][:, j], start=(kc == 0 and j == 0),
                                                    stop=(kc == KX - 1 and j == EK - 1), skip_group_check=True)
                    last.then_inc(used, 1)

            def turn_hidden(u):
                pe.wait_ge(h_done, u + 2)
                for j in range(EK):
                    last = nc.tensor.transpose(ps[:, 0, j * P:(j + 1) * P], hh[:, j * P:(j + 1) * P], ident)
                last.then_inc(htr_done, 1)
                pe.wait_ge(ht_ready, u + 1)

            def down(u, c):
                l = 2 * KX + c
                landed(u, 2 * l)
                landed(u, 2 * l + 1)
                pe.wait_ge(y_split, u * DX + (c + 1))
                for j in range(EK):
                    for ab in range(2):
                        last = nc.tensor.matmul(ps[HALF[ab], 2 + c % 2], ht[:, j, HALF[ab]], ring[(2 * l + ab) % RING][:, j],
                                                start=(j == 0), stop=(j == EK - 1), skip_group_check=True)
                last.then_inc(used, 1)

            def combine(u, c):
                pe.wait_ge(y_split, u * DX + (c + 3))
                for n in range(NT):
                    pe.wait_ge(add_done, u * (DX * NT) + (c * NT + n + 1))
                    nc.tensor.matmul(ps[:, 4 + n % 2], selt[:, n], yh[:, c % 2], start=True, stop=False)
                    nc.tensor.matmul(ps[:, 4 + n % 2], selt[:, n], yl[:, c % 2], start=False, stop=True).then_inc(cb_done, 1)

            def back(u):
                pe.wait_ge(selt_done, u + 1)
                down(u, 0)
                for c in range(1, DX):
                    down(u, c)
                    combine(u, c - 1)
                combine(u, DX - 1)

            pe.wait_ge(xr_done, 2 * NT)
            pe.wait_ge(xb0_ready, NT)
            pe.wait_ge(xb1_ready, NT)
            pe.wait_ge(table_ready, 1)
            gather(0)
            with pe.Fori(0, PAIRS - 1) as u:
                turn_selection(u)
                gate_up(u)
                pe.wait_ge(selt_done, u + 1)
                gather(u + 1)
                turn_hidden(u)
                back(u)
            turn_selection(PAIRS - 1)
            gate_up(PAIRS - 1)
            turn_hidden(PAIRS - 1)
            back(PAIRS - 1)
            n_over = pe.value_load(over_n[0:1, 0:1], min_val=0, max_val=MAX_OVER - 1)
            with pe.Fori(0, MAX_OVER - 1) as i:
                with pe.If(i < n_over):
                    u = i + PAIRS
                    gather(u)
                    turn_selection(u)
                    gate_up(u)
                    turn_hidden(u)
                    back(u)

        @block.vector
        def _(dve):
            for s, credit in CREDITS:
                dve.sem_inc(s, credit)
            step = [0]

            def link(ins):
                step[0] += 1
                ins.then_inc(dve_step, 1)
                dve.wait_ge(dve_step, step[0])

            def finish_root(n):
                nc.vector.reciprocal(rvar[:], var[:]).then_inc(rvar_ready, 1)
                dve.wait_ge(root_done, n)
                link(nc.vector.tensor_tensor(rvar[:], rstd[:], rstd[:], ALU.mult))
                link(nc.vector.tensor_tensor(rvar[:], rvar[:], var[:], ALU.mult))
                link(nc.vector.tensor_scalar(rvar[:], rvar[:], -0.5, 1.5, ALU.mult, ALU.add))
                link(nc.vector.tensor_tensor(rstd[:], rstd[:], rvar[:], ALU.mult))

            dve.wait_ge(const_in, 16)
            nc.vector.tensor_copy(constb[:].rearrange("p a b -> p (a b)"), wide).then_inc(constb_ready, 1)
            dve.wait_ge(sq_done, NT)
            link(nc.vector.tensor_scalar(var[:], sumsq[:], 1.0 / D, EPS, ALU.mult, ALU.add))
            finish_root(1)
            dve.wait_ge(g1_in, 16)
            for m in range(NT):
                nc.vector.scalar_tensor_tensor(out=xnat[:, m], in0=xnat[:, m], scalar=rstd[:, m:m + 1], in1=g1bc[:],
                                               op0=ALU.mult, op1=ALU.mult).then_inc(xn_ready, 1)
            for t in range(NT * KT // 4):
                m, kc = t // (KT // 4), t % (KT // 4)
                dve.wait_ge(tr_hi, t + 1)
                dst = slice(4 * kc, 4 * kc + 4), slice(m * P, (m + 1) * P)
                nc.vector.tensor_tensor(xl[:, dst[0], dst[1]], ps[:, 4 + t % 4].rearrange("p (k n) -> p k n", k=4),
                                        xh[:, dst[0], dst[1]].bitcast(F32), ALU.subtract).then_inc(tr_lo, 1)
            dve.wait_ge(wst_tr, 1)
            nc.vector.tensor_copy(wst[:].rearrange("p g t -> p (g t)"), ps[:, 0:2].rearrange("p a b -> p (a b)")
                                  ).then_inc(wst_ready, 1)

            for m in range(NT):
                dve.wait_ge(v_gelu, NT * (WB - 1) + m + 1)
                for b in range(WB):
                    last = nc.vector.bn_stats(bnst[:, m, b], v[:, m, b * CB:(b + 1) * CB])
                link(last)
                link(nc.vector.bn_aggr(bnag[:, m], bnst[:, m].rearrange("p a b -> p (a b)")))
            link(nc.vector.tensor_scalar(var[:], bnag[:, :, 1:2].rearrange("p m o -> p (m o)"), EPS, None, ALU.add))
            finish_root(2)
            dve.wait_ge(small_in, 16 * N_SMALL)
            for m in range(NT):
                link(nc.vector.tensor_scalar(v[:, m], v[:, m], bnag[:, m, 0:1], rstd[:, m:m + 1], ALU.subtract, ALU.mult))
                link(nc.vector.tensor_tensor(v[:, m], v[:, m], lng[:], ALU.mult))
                nc.vector.tensor_tensor(v[:, m], v[:, m], lnb[:], ALU.add).then_inc(v_ready, 1)
            nc.vector.memset(xc[:, :, 0:2], 0.0).then_inc(pad_zero, 1)

            def chain_in(i, per, base):
                local = [0]

                def chain(ins):
                    local[0] += 1
                    ins.then_inc(dve_step, 1)
                    dve.wait_ge(dve_step, i * per + (base + local[0]))
                return chain

            CONV_STEPS = 4
            with dve.Fori(0, WB) as i:
                chain = chain_in(i, CONV_STEPS, step[0])
                q = i * 3 * KC + Q_CONV
                dve.wait_ge(pe_chunk, q + KC)
                for m in range(MB):
                    last = nc.vector.tensor_copy(cbuf[:, m], ps[:, m])
                last.then_inc(set_free[0], 1)
                dve.wait_ge(set_free[0], 2 * i + 2)
                dve.wait_ge(pe_chunk, q + 2 * KC)
                dve.wait_ge(pad_zero, 1)
                for m in range(MB):
                    last = nc.vector.tensor_tensor(xc[:, m, 2:N + 2], ps[:, 4 + m], cbuf[:, m], ALU.mult)
                last.then_inc(set_free[1], 1)
                dve.wait_ge(set_free[1], i + 2)
                for k in (2, 1, 0):
                    for m in range(MB):
                        w = convw[:, k, bass.ds(i * MB + m, 1)]
                        if k == 2:
                            last = nc.vector.tensor_scalar(cbuf[:, m], xc[:, m, 2:N + 2], w, None, ALU.mult)
                        else:
                            last = nc.vector.scalar_tensor_tensor(out=cbuf[:, m], in0=xc[:, m, k:k + N], scalar=w,
                                                                  in1=cbuf[:, m], op0=ALU.mult, op1=ALU.add)
                    chain(last)
                dve.wait_ge(pe_chunk, q + 3 * KC)
                for m in range(MB):
                    last = nc.vector.tensor_tensor(cbuf[:, m], ps[:, m], cbuf[:, m], ALU.mult)
                last.then_inc(set_free[0], 1)
                dve.wait_ge(set_free[0], 2 * i + 3)
                mine = bass.ds(i * MB, MB)
                chain(nc.vector.tensor_copy(yah[:, mine], cbuf[:]))
                nc.vector.tensor_tensor(yal[:, mine], cbuf[:], yah[:, mine].bitcast(F32), ALU.subtract
                                        ).then_inc(ya_ready, 1)
                dve.wait_ge(ya_ready, i + 1)
            step[0] += WB * CONV_STEPS

            SGU_STEPS = 1
            with dve.Fori(0, WB) as i:
                chain = chain_in(i, SGU_STEPS, step[0])
                dve.wait_ge(mixed_done, i + 1)
                for m in range(MB):
                    bias = sgub[:, bass.ds(i * MB + m, 1)].to_broadcast([P, NT, P])
                    last = nc.vector.tensor_tensor(mx[:, m].rearrange("p (n t) -> p n t", n=NT),
                                                   ps[:, 4 + m].rearrange("p (n t) -> p n t", n=NT), bias, ALU.add)
                last.then_inc(set_free[1], 1)
                dve.wait_ge(set_free[1], i + (WB + 2))
                dve.wait_ge(u_ready, MB * i + MB)
                nc.vector.tensor_tensor(mx[:], mx[:], sg[:], ALU.mult).then_inc(u_used, 1)
                dve.wait_ge(u_used, i + 2)
                mine = bass.ds(i * MB, MB)
                chain(nc.vector.tensor_copy(ybh[:, mine], mx[:]))
                nc.vector.tensor_tensor(ybl[:, mine], mx[:], ybh[:, mine].bitcast(F32), ALU.subtract
                                        ).then_inc(yb_ready, 1)
                dve.wait_ge(yb_ready, i + 1)
            step[0] += WB * SGU_STEPS

            with dve.Fori(0, DB) as i:
                mine = bass.ds(i * MB, MB)
                for r in range(2):
                    dve.wait_ge(pe_chunk, i * 2 * (KC + WC) + (Q_MERGE + (r + 1) * (KC + WC)))
                    dve.wait_ge(sg_ready, i * 2 * MB + (MB * (r + 1) + 1))
                    if r == 0:
                        nc.vector.tensor_tensor(mrg[:, mine], ps[:, 4:8], sg[:], ALU.mult).then_inc(set_free[1], 1)
                    else:
                        nc.vector.tensor_tensor(sg[:], ps[:, 4:8], sg[:], ALU.mult).then_inc(set_free[1], 1)
                        dve.wait_ge(set_free[1], i * 2 + (2 * WB + 3))
                        nc.vector.tensor_tensor(mrg[:, mine], mrg[:, mine], sg[:], ALU.add).then_inc(mrg_sum, 1)
                        dve.wait_ge(mrg_sum, i + 2)
            for k in range(KT):
                link(nc.vector.tensor_copy(mh[:, k], mrg[:, k]))
                nc.vector.tensor_tensor(ml[:, k], mrg[:, k], mh[:, k].bitcast(F32), ALU.subtract).then_inc(m_ready, 1)
            dve.wait_ge(h_in, 16)
            with dve.Fori(0, DB // 2) as i:
                for s in range(2):
                    dve.wait_ge(pe_chunk, i * 2 * KC + (Q_OUT + (s + 1) * KC))
                    for m in range(NT):
                        hs = h[:, m, bass.ds(i * 2 * CB + s * CB, CB)]
                        nc.vector.tensor_tensor(hs, hs, ps[:, 4 * s + m], ALU.add).then_inc(h_ready[s], 1)

            dve.wait_ge(sq_done, 2 * NT)
            link(nc.vector.tensor_scalar(var[:], sumsq[:], 1.0 / D, EPS, ALU.mult, ALU.add))
            finish_root(3)
            dve.wait_ge(g2_in, 16)
            for m in range(NT):
                nc.vector.scalar_tensor_tensor(out=xn[:, m], in0=h[:, m], scalar=rstd[:, m:m + 1], in1=g2bc[:],
                                               op0=ALU.mult, op1=ALU.mult).then_inc(xn2_ready, 1)
            for m in range(NT):
                dve.wait_ge(xb0_ready, m + 1)
                dve.wait_ge(xt_done, (m + 1) * (KT // 4))
                nc.vector.tensor_tensor(xn[:, m], xn[:, m], xb[:, 0, m], ALU.subtract).then_inc(xr_done, 1)
                dve.wait_ge(xb1_ready, m + 1)
                nc.vector.tensor_tensor(xb[:, 2, m], xn[:, m], xb[:, 1, m], ALU.subtract).then_inc(xr_done, 1)
            dve.wait_ge(router_in, 32)
            dve.wait_ge(logit_done, NT)
            for m in range(NT):
                last = nc.vector.tensor_tensor(lg[:, m], ps[:, m, 0:EG + E], rb[:], ALU.add)
            link(last)

            def wide_n(ap, k):
                return ap.to_broadcast([P, NT, k])

            def top(dst, code, best):
                link(nc.vector.tensor_reduce(best[:], code[:], AX, ALU.max))
                link(nc.vector.tensor_tensor(dst[:], code[:], wide_n(best[:], code.shape[2]), ALU.is_equal))

            gl = lg[:, :, 0:EG]
            link(nc.vector.tensor_reduce(gmax[:], gl, AX, ALU.max))
            nc.vector.tensor_tensor(gsh[:], gl, wide_n(gmax[:], EG), ALU.subtract).then_inc(gsh_ready, 1)
            dve.wait_ge(gsh_ready, 1)
            link(nc.vector.scalar_tensor_tensor(out=gcode[:], in0=gsh[:], scalar=0.0, in1=desc_g.unsqueeze(1).to_broadcast([P, NT, EG]),
                                                op0=ALU.is_ge, op1=ALU.mult))
            top(goh, gcode, gtop)
            link(nc.vector.tensor_tensor(emask[:], lg[:, :, EG:].rearrange("p n (g e) -> p n g e", g=EG),
                                         goh[:].unsqueeze(3).to_broadcast([P, NT, EG, EPG]), ALU.mult))
            link(nc.vector.tensor_reduce(esel[:], emask[:].rearrange("p n g e -> p n e g"), AX, ALU.add))
            link(nc.vector.tensor_reduce(emax[:], esel[:], AX, ALU.max))
            nc.vector.tensor_tensor(esh[:], esel[:], wide_n(emax[:], EPG), ALU.subtract).then_inc(esh_ready, 1)
            dve.wait_ge(esh_ready, 1)
            de = desc_e.unsqueeze(1).to_broadcast([P, NT, EPG])
            link(nc.vector.scalar_tensor_tensor(out=ecode[:], in0=esh[:], scalar=0.0, in1=de, op0=ALU.is_ge, op1=ALU.mult))
            top(oh1, ecode, etop)
            link(nc.vector.scalar_tensor_tensor(out=es2[:], in0=oh1[:], scalar=-3.0e38, in1=esh[:], op0=ALU.mult, op1=ALU.add))
            link(nc.vector.tensor_reduce(emax[:], es2[:], AX, ALU.max))
            link(nc.vector.tensor_tensor(ecode[:], es2[:], wide_n(emax[:], EPG), ALU.is_equal))
            link(nc.vector.tensor_tensor(ecode[:], ecode[:], de, ALU.mult))
            top(oh2, ecode, etop)
            link(nc.vector.tensor_tensor(m8[:], oh1[:], oh2[:], ALU.add))
            dve.wait_ge(gexp_ready, 1)
            link(nc.vector.tensor_reduce(gsum[:], gexp[:], AX, ALU.add))
            link(nc.vector.reciprocal(gw[:], gsum[:]))
            dve.wait_ge(eexp_ready, 1)
            link(nc.vector.tensor_tensor(p8[:], eexp[:], m8[:], ALU.mult))
            link(nc.vector.tensor_reduce(den[:], p8[:], AX, ALU.add))
            link(nc.vector.reciprocal(rden[:], den[:]))
            link(nc.vector.tensor_tensor(rden[:], rden[:], gw[:], ALU.mult))
            link(nc.vector.tensor_tensor(p8[:], p8[:], wide_n(rden[:], EPG), ALU.mult))
            g4 = goh[:].unsqueeze(3).to_broadcast([P, NT, EG, EPG])
            link(nc.vector.tensor_tensor(w32[:].rearrange("p n (g e) -> p n g e", g=EG), g4,
                                         p8[:].unsqueeze(2).to_broadcast([P, NT, EG, EPG]), ALU.mult))
            link(nc.vector.tensor_tensor(m32[:], g4, m8[:].unsqueeze(2).to_broadcast([P, NT, EG, EPG]), ALU.mult))
            nc.vector.tensor_copy(m32b[:], m32[:].rearrange("p n g e -> p n (g e)"))
            link(nc.vector.tensor_reduce(msum[:], m32[:].rearrange("p n g e -> p (g e) n"), AX, ALU.add))
            nc.vector.tensor_copy(m128[:], msum[:].unsqueeze(2).to_broadcast([P, E, P // E])).then_inc(mask_ready, 1)

            dve.wait_ge(rank_done, 1)
            link(nc.vector.scalar_tensor_tensor(out=pos[:].rearrange("p n e -> p (n e)"), in0=ps[:, 4, 0:NT * E], scalar=1.0,
                                                in1=m32[:].rearrange("p n g e -> p (n g e)"), op0=ALU.add, op1=ALU.mult))
            link(nc.vector.tensor_scalar(pos[:], pos[:], -1.0, None, ALU.add))
            link(nc.vector.tensor_tensor(active[:], ps[:, 5, 0:1], const[:, 4 * P:4 * P + 1], ALU.is_gt))
            nc.vector.tensor_copy(activeb[:], active[:]).then_inc(active_ready, 1)
            dve.wait_ge(prefix_done, 1)
            link(nc.vector.tensor_copy(prefix[:], ps[:, 5, 2:3]))
            link(nc.vector.tensor_scalar(unit_oh[:], iota_u, prefix[:], active[:], ALU.is_equal, ALU.mult))
            nc.vector.tensor_copy(unit_ohb[:], unit_oh[:]).then_inc(unit_ready, 1)
            dve.wait_ge(table_done, 1)
            nc.vector.tensor_copy(over_e[:], ps[0:1, 6, 0:MAX_OVER])
            nc.vector.tensor_copy(over_r[:], ps[:, 6, MAX_OVER:2 * MAX_OVER])
            link(nc.vector.tensor_reduce(over_nf[:], ps[:, 6, 2 * MAX_OVER:3 * MAX_OVER], AX, ALU.add))
            nc.vector.tensor_copy(over_n[:], over_nf[0:1]).then_inc(table_ready, 1)
            dve.wait_ge(table_ready, 1)

            def select(link_):
                link_(nc.vector.tensor_tensor(self_[:].rearrange("p n (h c) -> p n h c", h=2),
                                              iota_c.unsqueeze(1).unsqueeze(1).to_broadcast([P, NT, 2, CAP]),
                                              pc[:].unsqueeze(3).to_broadcast([P, NT, 2, CAP]), ALU.is_equal))
                nc.vector.tensor_copy(selb[:], self_[:]).then_inc(sel_ready, 1)

            def take_selection(u):
                dve.wait_ge(seltr_done, u + 1)
                nc.vector.tensor_copy(selt[:].rearrange("p n t -> p (n t)"), ps[:, 6])
                nc.vector.tensor_copy(wsl[0:CAP], ps[0:CAP, 7, 0:1])
                nc.vector.tensor_copy(wsl[CAP:], ps[CAP:, 7, 1:2]).then_inc(selt_done, 1)

            def hidden(u):
                dve.wait_ge(silu_done, u + 1)
                dve.wait_ge(used, u * USED + 2 * KX)
                dve.wait_ge(selt_done, u + 1)
                nc.vector.scalar_tensor_tensor(out=hh[:], in0=ps[:, 1], scalar=wsl[:], in1=sl[:], op0=ALU.mult,
                                               op1=ALU.mult).then_inc(h_done, 1)

            def take_hidden(u):
                dve.wait_ge(htr_done, u + 1)
                nc.vector.tensor_copy(ht[:].rearrange("p j s -> p (j s)"), ps[:, 0]).then_inc(ht_ready, 1)

            def low_y(u, c):
                dve.wait_ge(yh_done, u * DX + (c + 1))
                nc.vector.tensor_tensor(yl[:, c % 2], ps[:, 2 + c % 2], yh[:, c % 2].bitcast(F32), ALU.subtract
                                        ).then_inc(y_split, 1)

            def add(u, c):
                for n in range(NT):
                    dve.wait_ge(cb_done, u * (DX * NT) + (c * NT + n + 6))
                    hs = h[:, n, c * CB:(c + 1) * CB]
                    nc.vector.tensor_tensor(hs, hs, ps[:, 4 + n % 2], ALU.add).then_inc(add_done, 1)

            def back(u):
                hidden(u)
                take_hidden(u)
                low_y(u, 0)
                for c in range(1, DX):
                    low_y(u, c)
                    add(u, c - 1)
                add(u, DX - 1)

            nc.vector.tensor_copy(pc[:], pos[:, :, 0:2])
            link(nc.vector.tensor_copy(wc[:], w32[:, :, 0:2]))
            select(link)
            SEL_STEPS = 2
            with dve.Fori(0, PAIRS - 1) as u:
                chain = chain_in(u, SEL_STEPS, step[0])
                take_selection(u)
                nc.vector.tensor_copy(pc[:], pos[:, :, bass.ds(u * 2 + 2, 2)])
                chain(nc.vector.tensor_copy(wc[:], w32[:, :, bass.ds(u * 2 + 2, 2)]))
                select(chain)
                back(u)
            step[0] += (PAIRS - 1) * SEL_STEPS
            take_selection(PAIRS - 1)
            back(PAIRS - 1)
            dve.wait_ge(add_done, PAIRS * DX * NT + 2)

            n_over = dve.value_load(over_n[0:1, 0:1], min_val=0, max_val=MAX_OVER - 1)
            OVER_STEPS = 3
            with dve.Fori(0, MAX_OVER - 1) as i:
                with dve.If(i < n_over):
                    u = i + PAIRS
                    chain = chain_in(i, OVER_STEPS, step[0])
                    e = dve.value_load(over_e[0:1, bass.ds(i, 1)], min_val=0, max_val=E - 1)
                    for n in range(NT):
                        nc.vector.tensor_scalar(wc[:, n], w32[:, n, bass.ds(e, 1)].to_broadcast([P, 2]), 0.0, None, ALU.add)
                        last = nc.vector.tensor_scalar(pc[:, n, 0:1], pos[:, n, bass.ds(e, 1)],
                                                       over_r[:, bass.ds(i, 1)], None, ALU.subtract)
                    chain(last)
                    chain(nc.vector.tensor_scalar(pc[:, :, 1:2], pc[:, :, 0:1], -float(CAP), None, ALU.add))
                    select(chain)
                    take_selection(u)
                    back(u)
            dve.wait_ge(add_done, n_over * (DX * NT) + (PAIRS * DX * NT + 2))
            nc.vector.memset(prefix[:], 0.0).then_inc(moe_done, 1)
            step_end = sem("step_end")
            dve.wait_ge(sq_done, 3 * NT)
            nc.vector.tensor_scalar(var[:], sumsq[:], 1.0 / D, EPS, ALU.mult, ALU.add).then_inc(step_end, 1)
            dve.wait_ge(step_end, 1)
            nc.vector.reciprocal(rvar[:], var[:]).then_inc(rvar_ready, 1)
            dve.wait_ge(root_done, 4)
            nc.vector.tensor_tensor(rvar[:], rstd[:], rstd[:], ALU.mult).then_inc(step_end, 1)
            dve.wait_ge(step_end, 2)
            nc.vector.tensor_tensor(rvar[:], rvar[:], var[:], ALU.mult).then_inc(step_end, 1)
            dve.wait_ge(step_end, 3)
            nc.vector.tensor_scalar(rvar[:], rvar[:], -0.5, 1.5, ALU.mult, ALU.add).then_inc(step_end, 1)
            dve.wait_ge(step_end, 4)
            nc.vector.tensor_tensor(rstd[:], rstd[:], rvar[:], ALU.mult).then_inc(step_end, 1)
            dve.wait_ge(step_end, 5)
            dve.wait_ge(fg_in, 16)
            for m in range(NT):
                nc.vector.scalar_tensor_tensor(out=h[:, m], in0=h[:, m], scalar=rstd[:, m:m + 1], in1=fgbc[:],
                                               op0=ALU.mult, op1=ALU.mult).then_inc(out_ready, 1)


def mixer_stream(w_in, w_branch, w_out):
    import numpy as np
    D, W = w_in.shape[0], w_branch.shape[1]
    blocks = []
    for i in range(W // CB):
        blocks.append((w_in, 4 * W + i * CB))
    for i in range(W // CB):
        blocks += [(w_in, b * W + i * CB) for b in (0, 2, 1)]
    for i in range(W // CB):
        blocks.append((w_in, 3 * W + i * CB))
    for i in range(D // CB):
        for r in range(w_branch.shape[0]):
            blocks += [(w_in, 5 * W + r * D + i * CB), (w_branch[r], i * CB)]
    for i in range(D // CB):
        blocks.append((w_out, i * CB))
    rows = CK * P
    stream = np.empty((sum(w.shape[0] // rows for w, _ in blocks), P, CK * CB), w_in.dtype)
    q = 0
    for w, col in blocks:
        n = w.shape[0] // rows
        stream[q:q + n].reshape(n, P, CK, CB)[:] = w[:, col:col + CB].reshape(n, CK, P, CB).transpose(0, 2, 1, 3)
        q += n
    return stream


def expert_stream(w_gate, w_up, w_down):
    import numpy as np
    E, D, F = w_gate.shape
    KC, DC = D // (EK * P), D // CB
    stream = np.empty((E, 2 * KC + DC, P, EK, CB), w_gate.dtype)
    stream[:, 0:2 * KC:2] = w_gate.reshape(E, KC, EK, P, F).transpose(0, 1, 3, 2, 4)
    stream[:, 1:2 * KC:2] = w_up.reshape(E, KC, EK, P, F).transpose(0, 1, 3, 2, 4)
    stream[:, 2 * KC:] = w_down.reshape(E, EK, P, DC, CB).transpose(0, 3, 2, 1, 4)
    return stream.reshape(E * (2 * KC + DC), P, EK * CB)


def shape_constants(EG, E):
    import numpy as np
    c = np.arange(P)
    per = P // E
    parts = [np.eye(P), c[:, None] < c[None, :], np.ones((P, P)),
             np.repeat(c[:, None] // per, P, axis=1),
             np.repeat(CAP + 2 * CAP * (c[:, None] % per), P, axis=1),
             np.tile(np.arange(CAP), (P, 1)), np.tile(np.arange(MAX_OVER), (P, 1)),
             np.tile(np.arange(EG, 0, -1), (P, 1)), np.tile(np.arange(E // EG, 0, -1), (P, 1))]
    return np.concatenate(parts, axis=1).astype(np.float32)


def kernel(x, norm1_g, w_in, b_gate, conv_w, ln_v_g, ln_v_b, sgu_w, sgu_b, w_branch, w_out,
           norm2_g, router_g, router_g_b, router_e, router_e_b, w_gate, w_up, w_down, final_g):
    import numpy as _np
    import concourse.bacc as _bacc
    from concourse import mybir as _mybir
    from concourse.bass_utils import run_bass_kernel_spmd as _run

    assert w_in.shape[0] == 1
    D = x.shape[2]
    laid = {
        'x': x,
        'norm1_g': norm1_g,
        'mixer_w': mixer_stream(w_in[0], w_branch[0], w_out[0]),
        'b_gate': b_gate[0].reshape(-1, P).T,
        'conv_w': conv_w[0].reshape(conv_w.shape[1], -1, P).transpose(2, 0, 1),
        'ln_v_g': ln_v_g, 'ln_v_b': ln_v_b, 'sgu_w': sgu_w, 'sgu_b': sgu_b,
        'norm2_g': norm2_g,
        'router_w': _np.concatenate([router_g[0], router_e[0]], axis=1).reshape(D // P, P, -1).transpose(1, 0, 2),
        'router_b': _np.concatenate([router_g_b, router_e_b], axis=1),
        'expert_w': expert_stream(w_gate[0], w_up[0], w_down[0]),
        'final_g': final_g.reshape(1, -1),
        'consts': shape_constants(router_g.shape[2], router_e.shape[2]),
    }
    nc = _bacc.Bacc("TRN2", target_bir_lowering=False, num_devices=1)
    arrays, args = {}, []
    for name, a in laid.items():
        a = _np.ascontiguousarray(a)
        arrays[f"in_{name}_dram"] = a
        args.append(nc.dram_tensor(f"in_{name}_dram", a.shape, _mybir.dt.from_np(a.dtype), kind="ExternalInput").ap())
    args.append(nc.dram_tensor("out_0_dram", x.shape, _mybir.dt.from_np(_np.dtype('float32')), kind="ExternalOutput").ap())
    hybrid_block(nc, *args)
    r = _run(nc, [arrays], core_ids=[0])
    return r.results[0]["out_0_dram"]
```

```python
from contextlib import ExitStack

import concourse.bass as bass
from concourse import mybir

P = 128
F32 = mybir.dt.float32
F32R = mybir.dt.float32r
BF16 = mybir.dt.bfloat16
I32 = mybir.dt.int32
ALU = mybir.AluOpType
ACT = mybir.ActivationFunctionType
AX = mybir.AxisListType.X

EPS = 1e-6
CB = 512
CK = 2
RAW_SLOTS = 4
SPLIT_SLOTS = 2
EK = 4
CAP = 64
MAX_OVER = 16
RING = 8


def hybrid_block(nc, x, norm1_g, mixer_w, b_gate, conv_w, ln_v_g, ln_v_b, sgu_w, sgu_b,
                 norm2_g, router_w, router_b, expert_w, final_g, consts, out):
    _, N, D = x.shape
    W = ln_v_g.shape[1]
    G = sgu_w.shape[1]
    KT, NT, WT = D // P, N // P, W // P
    KC, WC = KT // CK, WT // CK
    DB, WB = D // CB, W // CB
    MB = CB // P
    assert NT == 4 and MB == 4 and sgu_w.shape[2] == P

    EG = 4
    E = router_w.shape[2] - EG
    EPG = E // EG
    PAIRS = E // 2
    assert CAP + (P // E) * 2 * CAP >= N and 2 * N // (CAP + 1) < MAX_OVER
    KX = D // (EK * P)
    DX = D // CB
    LX = 2 * KX + DX
    USED = LX
    assert 2 * LX % RING == 0 and EK * P == CB and MB == EK

    x_v = x[0].rearrange("(m p) d -> p m d", p=P)
    out_v = out[0].rearrange("(m p) d -> p m d", p=P)

    Q_V = 0
    Q_CONV = Q_V + WB * KC
    Q_U = Q_CONV + WB * 3 * KC
    Q_MERGE = Q_U + WB * KC
    Q_OUT = Q_MERGE + DB * 2 * (KC + WC)
    Q_END = Q_OUT + DB * KC

    with ExitStack() as ctx:
        def sb(name, shape, dt=F32):
            return ctx.enter_context(nc.sbuf_tensor(name, shape, dt))

        def sem(name):
            return ctx.enter_context(nc.semaphore(name))

        const = sb("const", [P, consts.shape[1]])
        ident, wide = const[:, 0:P], const[:, P:5 * P]
        iota_c = const[:, 5 * P:5 * P + CAP]
        iota_u = const[:, 5 * P + CAP:5 * P + CAP + MAX_OVER]
        desc_g = const[:, 5 * P + CAP + MAX_OVER:5 * P + CAP + MAX_OVER + EG]
        desc_e = const[:, 5 * P + CAP + MAX_OVER + EG:5 * P + CAP + MAX_OVER + EG + EPG]
        constb = sb("constb", [P, 4, P], BF16)
        before, ones, cand_e, cand_r = (constb[:, k] for k in range(4))
        pos = sb("pos", [P, NT, E])
        w32 = sb("w32", [P, NT, E])
        pc, wc = sb("pc", [P, NT, 2]), sb("wc", [P, NT, 2])
        wsl = sb("wsl", [P, 1])
        over_n, over_e = sb("over_n", [1, 1], I32), sb("over_e", [1, MAX_OVER], I32)
        over_r = sb("over_r", [P, MAX_OVER])
        bgate = sb("bgate", [P, 2 * KT])
        convw = sb("convw", [P, 3, WT])
        sumsq, sumsq2 = sb("sumsq", [P, NT]), sb("sumsq2", [P, NT])
        warm = sb("warm", [P, 4])
        rstd = sb("rstd", [P, NT])
        var = sb("var", [P, NT])
        rvar = sb("rvar", [P, NT])
        bnst = sb("bnst", [P, NT, 2, 6])
        bnag = sb("bnag", [P, NT, 2])

        BASE = 24544
        assert nc.sbuf_base <= BASE, nc.sbuf_base

        def at(name, shape, dt, kib):
            return nc.alloc_sbuf_tensor_at(name, shape, dt, offset=BASE + int(kib * 1024))

        xh, xl = at("xh", [P, KT, N], F32R, 0), at("xl", [P, KT, N], F32R, 32)
        mh, ml = at("mh", [P, KT, N], F32R, 0), at("ml", [P, KT, N], F32R, 32)
        yah, yal = at("yah", [P, WT, N], F32R, 64), at("yal", [P, WT, N], F32R, 80)
        ybh, ybl = at("ybh", [P, WT, N], F32R, 96), at("ybl", [P, WT, N], F32R, 112)
        xnat = at("xnat", [P, NT, D], F32, 64)
        g1bc = at("g1bc", [P, D], F32, 96)
        wsraw = at("wsraw", [P, G, P], F32, 104)
        cbuf = at("cbuf", [P, MB, N], F32, 96)
        xc = at("xc", [P, MB, N + 2], F32, 104)
        lng, lnb = at("lng", [P, W], F32, 116), at("lnb", [P, W], F32, 120)
        h = at("h", [P, NT, D], F32, 64)
        v = at("v", [P, NT, W], F32, 128)
        wst = at("wst", [P, G, P], F32, 144)
        sgub = at("sgub", [P, G, P], F32, 148)
        mx = at("mx", [P, MB, N], F32, 152)
        mrg = at("mrg", [P, KT, N], F32, 128)
        raw = at("raw", [P, RAW_SLOTS, CK, CB], F32, 160)
        wh = at("wh", [P, SPLIT_SLOTS, CK, CB], F32R, 176)
        wl = at("wl", [P, SPLIT_SLOTS, CK, CB], F32R, 184)
        sg = at("sg", [P, MB, N], F32, 192)

        ring = [at(f"ring{s}", [P, EK, CB], F32, 96 + 8 * s) for s in range(RING)]
        xn = at("xn", [P, NT, D], F32, 160)
        g2bc = at("g2bc", [P, D], F32, 40)
        xb = at("xb", [P, 3, NT, D], BF16, 0)
        xt = at("xt", [P, 2, KT, P], F32, 48)
        xg = [at("xg0", [P, KT, P], F32, 48), at("xg1", [P, KT, P], F32, 184)]
        hh, sl = at("hh", [P, CB], F32, 56), at("sl", [P, CB], F32, 58)
        ht = at("ht", [P, EK, P], F32, 60)
        selb = at("selb", [P, NT, P], BF16, 62)
        self_ = at("self_", [P, NT, P], F32, 160)
        selt = at("selt", [P, NT, P], F32R, 162)
        yh, yl = at("yh", [P, 2, CB], F32R, 164), at("yl", [P, 2, CB], F32R, 168)
        fgbc = at("fgbc", [P, D], F32, 176)
        place = [192 * 1024]

        def rt(name, shape, dt=F32):
            t = nc.alloc_sbuf_tensor_at(name, shape, dt, offset=BASE + place[0])
            n = 4 if dt == F32 else 2
            for k in shape[1:]:
                n *= k
            place[0] += (n + 31) // 32 * 32
            assert place[0] <= 200 * 1024 - 64
            return t

        rw = rt("rw", [P, KT, EG + E])
        rb = rt("rb", [P, EG + E])
        lg = rt("lg", [P, NT, EG + E])
        gmax, gsum, gw, gtop = (rt(n, [P, NT, 1]) for n in ("gmax", "gsum", "gw", "gtop"))
        gsh, gexp, gcode, goh = (rt(n, [P, NT, EG]) for n in ("gsh", "gexp", "gcode", "goh"))
        emask = rt("emask", [P, NT, EG, EPG])
        esel, esh, eexp, ecode, oh1, es2, oh2, m8, p8 = (
            rt(n, [P, NT, EPG]) for n in ("esel", "esh", "eexp", "ecode", "oh1", "es2", "oh2", "m8", "p8"))
        emax, etop, den, rden = (rt(n, [P, NT, 1]) for n in ("emax", "etop", "den", "rden"))
        m32 = rt("m32", [P, NT, EG, EPG])
        m32b = rt("m32b", [P, NT, E], BF16)
        msum = rt("msum", [P, E])
        m128 = rt("m128", [P, E, P // E], BF16)
        active = rt("active", [P, 1])
        activeb = rt("activeb", [P, 1], BF16)
        prefix = rt("prefix", [P, 1])
        unit_oh = rt("unit_oh", [P, MAX_OVER])
        unit_ohb = rt("unit_ohb", [P, MAX_OVER], BF16)
        over_nf = rt("over_nf", [P, 1])

        ps = ctx.enter_context(nc.psum_tensor("ps", [P, 8, CB], F32))

        x_in = [sem(f"x_in{m}") for m in range(NT)]
        g1_in = sem("g1_in")
        ws_in = sem("ws_in")
        small_in = sem("small_in")
        h_in = sem("h_in")
        raw_in = [sem(f"raw_in{s}") for s in range(RAW_SLOTS)]
        const_in, router_in, constb_ready = sem("const_in"), sem("router_in"), sem("constb_ready")
        warm_ready = sem("warm_ready")
        sq_done, rvar_ready, root_done, xn_ready = sem("sq_done"), sem("rvar_ready"), sem("root_done"), sem("xn_ready")
        tr_done, tr_hi, tr_lo = sem("tr_done"), sem("tr_hi"), sem("tr_lo")
        ws_masked, wst_tr, wst_ready = sem("ws_masked"), sem("wst_tr"), sem("wst_ready")
        hi_done, lo_done, pe_chunk = sem("hi_done"), sem("lo_done"), sem("pe_chunk")
        set_free = [sem("set_free0"), sem("set_free1")]
        v_gelu, v_ready = sem("v_gelu"), sem("v_ready")
        pad_zero = sem("pad_zero")
        ya_ready, yb_ready = sem("ya_ready"), sem("yb_ready")
        mixed_done, u_ready, u_used = sem("mixed_done"), sem("u_ready"), sem("u_used")
        sg_ready, mrg_sum = sem("sg_ready"), sem("mrg_sum")
        m_ready, h_ready = sem("m_ready"), [sem("h_ready0"), sem("h_ready1")]
        g2_in, fg_in = sem("g2_in"), sem("fg_in")
        xn2_ready, xb0_ready, xt_done, xt_ready, xb1_ready, xb2_ready, xr_done = (
            sem(n) for n in ("xn2_ready", "xb0_ready", "xt_done", "xt_ready", "xb1_ready", "xb2_ready", "xr_done"))
        logit_done, gsh_ready, gexp_ready, esh_ready, eexp_ready = (
            sem(n) for n in ("logit_done", "gsh_ready", "gexp_ready", "esh_ready", "eexp_ready"))
        mask_ready, rank_done, active_ready, prefix_done, unit_ready, table_done, table_ready = (
            sem(n) for n in ("mask_ready", "rank_done", "active_ready", "prefix_done", "unit_ready", "table_done",
                             "table_ready"))
        ring_in = [sem(f"ring_in{s}") for s in range(RING)]
        sel_ready, gat_done, xg_done, seltr_done, selt_done = (
            sem(n) for n in ("sel_ready", "gat_done", "xg_done", "seltr_done", "selt_done"))
        used, silu_done, h_done, htr_done, ht_ready = (
            sem(n) for n in ("used", "silu_done", "h_done", "htr_done", "ht_ready"))
        yh_done, y_split, cb_done, add_done, moe_done = (
            sem(n) for n in ("yh_done", "y_split", "cb_done", "add_done", "moe_done"))
        out_ready = sem("out_ready")
        dve_step = sem("dve_step")
        stored = sem("stored")

        CREDITS = ((set_free[0], 1), (set_free[1], 1), (u_used, 1), (mrg_sum, 1), (sg_ready, 1), (h_ready[0], 1),
                   (h_ready[1], 1), (xg_done, 2), (y_split, 2), (add_done, NT), (cb_done, 5), (h_done, 1))

        block = ctx.enter_context(nc.Block())

        N_SMALL = 5

        @block.sync
        def _(sp):
            for m in range(NT):
                sp.dma_start(xnat[:, m], x_v[:, m]).then_inc(x_in[m], 16)
                if m == 0:
                    sp.dma_start(g1bc[:], norm1_g.partition_broadcast(P).rearrange("p o d -> p (o d)")).then_inc(g1_in, 16)

            def chunk(q, s):
                sp.dma_start(raw[:, s], mixer_w[bass.ds(q, 1)].rearrange("o p f -> (o p) f")).then_inc(raw_in[s], 16)

            for s in range(RAW_SLOTS):
                chunk(s, s)
            with sp.Fori(1, Q_OUT // RAW_SLOTS) as i:
                for s in range(RAW_SLOTS):
                    sp.wait_ge(lo_done, i * RAW_SLOTS + (s - RAW_SLOTS + 1))
                    chunk(i * RAW_SLOTS + s, s)
            def out_chunks(i):
                for s in range(RAW_SLOTS):
                    sp.wait_ge(lo_done, i * RAW_SLOTS + (s - RAW_SLOTS + 1))
                    chunk(i * RAW_SLOTS + s, s)

            def expert_chunk(q, s):
                sp.dma_start(ring[s][:].rearrange("p j n -> p (j n)"),
                             expert_w[bass.ds(q, 1)].rearrange("o p f -> (o p) f")).then_inc(ring_in[s], 16)

            lead, tail = Q_OUT // RAW_SLOTS + 2, Q_END // RAW_SLOTS - 2
            out_chunks(Q_OUT // RAW_SLOTS)
            sp.wait_ge(pe_chunk, Q_OUT)
            for m in range(NT):
                sp.dma_start(h[:, m], x_v[:, m]).then_inc(h_in, 16)
                if m == NT // 2 - 1:
                    out_chunks(Q_OUT // RAW_SLOTS + 1)
            sp.wait_ge(m_ready, KT)
            for i in range(lead, tail):
                out_chunks(i)
                for c in (2 * (i - lead), 2 * (i - lead) + 1):
                    expert_chunk((c % 2) * LX + c // 2, c)
            with sp.Fori(tail, Q_END // RAW_SLOTS) as i:
                out_chunks(i)
            sp.wait_ge(pe_chunk, Q_END)
            sp.dma_start(g2bc[:], norm2_g.partition_broadcast(P).rearrange("p o d -> p (o d)")).then_inc(g2_in, 16)

            def unit_chunks(u, first, last, expert):
                for c in range(first, last):
                    sp.wait_ge(used, u * USED + (c // 2 - RING // 2 + 1))
                    expert_chunk(expert(c % 2) * LX + c // 2, c % RING)

            with sp.Fori(0, PAIRS - 1) as u:
                unit_chunks(u, RING, 2 * LX, lambda ab: u * 2 + ab)
                unit_chunks(u + 1, 0, RING, lambda ab: u * 2 + (2 + ab))
            for c in range(RING, 2 * LX):
                sp.wait_ge(used, (PAIRS - 1) * USED + c // 2 - RING // 2 + 1)
                expert_chunk((E - 2 + c % 2) * LX + c // 2, c % RING)
            sp.wait_ge(sel_ready, 1)
            sp.dma_start(fgbc[:], final_g.partition_broadcast(P).rearrange("p o d -> p (o d)")).then_inc(fg_in, 16)
            sp.wait_ge(table_ready, 1)
            n_over = sp.value_load(over_n[0:1, 0:1], min_val=0, max_val=MAX_OVER - 1)
            with sp.Fori(0, MAX_OVER - 1) as i:
                with sp.If(i < n_over):
                    e = sp.value_load(over_e[0:1, bass.ds(i, 1)], min_val=0, max_val=E - 1)
                    for l in range(LX):
                        sp.wait_ge(used, (i + PAIRS) * USED + (l - RING // 2 + 1))
                        expert_chunk(e * LX + l, 2 * l % RING)
            for m in range(NT):
                sp.wait_ge(out_ready, m + 1)
                sp.dma_start(out_v[:, m], h[:, m]).then_inc(stored, 16)
            sp.wait_ge(stored, 16 * NT)

        @block.gpsimd
        def _(pool):
            pool.wait_ge(ws_in, 16)
            nc.gpsimd.affine_select(out=wsraw[:], in_=wsraw[:], compare_op=ALU.is_ge, fill=0.0, base=0,
                                    pattern=[[0, G], [-1, P]], channel_multiplier=1).then_inc(ws_masked, 1)

            with pool.Fori(0, Q_END // RAW_SLOTS) as i:
                for c in range(RAW_SLOTS):
                    pool.wait_ge(hi_done, i * RAW_SLOTS + c + 1)
                    s = c % SPLIT_SLOTS
                    nc.gpsimd.tensor_tensor(wl[:, s], raw[:, c], wh[:, s].bitcast(F32), ALU.subtract).then_inc(lo_done, 1)

            for m in range(NT):
                pool.wait_ge(xb1_ready, m + 1)
                nc.gpsimd.tensor_tensor(xb[:, 2, m], xn[:, m], xb[:, 1, m], ALU.subtract).then_inc(xb2_ready, 1)

        @block.scalar
        def _(act):
            act.dma_start(const[:], consts).then_inc(const_in, 16)
            act.dma_start(wsraw[:], sgu_w[0].rearrange("g t s -> t g s")).then_inc(ws_in, 16)

            def preload(func, k):
                act.wait_ge(warm_ready, 1)
                nc.scalar.activation(warm[:, k:k + 1], warm[:, 0:1], func)

            def square(m, cols, acc, n):
                if n > 1:
                    act.wait_ge(sq_done, n - 1)
                nc.scalar.activation(ps[:, 0:4].rearrange("p a b -> p (a b)")[:, 0:cols.shape[1]], cols, ACT.Square,
                                     accum_out=acc[:, m:m + 1]).then_inc(sq_done, 1)

            def root(m, n):
                act.wait_ge(rvar_ready, n)
                nc.scalar.activation(rstd[:, m], rvar[:, m], ACT.Sqrt).then_inc(root_done, 1)

            def turned(m):
                for kc in range(KT // 4):
                    t = m * (KT // 4) + kc
                    act.wait_ge(tr_done, t + 1)
                    nc.scalar.activation(xh[:, 4 * kc:4 * kc + 4, m * P:(m + 1) * P],
                                         ps[:, 4 + t % 4].rearrange("p (k n) -> p k n", k=4), ACT.Copy).then_inc(tr_hi, 1)

            def hi(q, c):
                if isinstance(q, int):
                    use = (q + c) // RAW_SLOTS + 1
                else:
                    use = q // RAW_SLOTS + c // RAW_SLOTS + 1
                act.wait_ge(raw_in[c % RAW_SLOTS], use * 16)
                if not isinstance(q, int) or q + c >= SPLIT_SLOTS:
                    act.wait_ge(pe_chunk, q + c - SPLIT_SLOTS + 1)
                nc.scalar.activation(wh[:, c % SPLIT_SLOTS], raw[:, c % RAW_SLOTS], ACT.Copy).then_inc(hi_done, 1)

            def hi_at(i, q0, per, c):
                act.wait_ge(raw_in[c % RAW_SLOTS], i * (16 * per // RAW_SLOTS) + 16 * ((q0 + c) // RAW_SLOTS + 1))
                act.wait_ge(pe_chunk, i * per + (q0 + c - SPLIT_SLOTS + 1))
                nc.scalar.activation(wh[:, c % SPLIT_SLOTS], raw[:, c % RAW_SLOTS], ACT.Copy).then_inc(hi_done, 1)

            preload(ACT.Sqrt, 1)
            for m in range(NT):
                act.wait_ge(x_in[m], 16)
                square(m, xnat[:, m], sumsq, m + 1)
                root(slice(m, m + 1), m + 1)
                if m == NT - 1:
                    act.dma_start(bgate[:], b_gate).then_inc(small_in, 16)
                    act.dma_start(convw[:], conv_w).then_inc(small_in, 16)
                    act.dma_start(lng[:], ln_v_g.partition_broadcast(P).rearrange("p o d -> p (o d)")).then_inc(small_in, 16)
                    act.dma_start(lnb[:], ln_v_b.partition_broadcast(P).rearrange("p o d -> p (o d)")).then_inc(small_in, 16)
                    act.dma_start(sgub[:], sgu_b.partition_broadcast(P).rearrange("p o g t -> p (o g) t")).then_inc(small_in, 16)
                if m >= 1:
                    turned(m - 1)
            hi(0, 0)
            turned(NT - 1)
            hi(0, 1)
            for i in range(WB):
                for c in range(KC):
                    hi(Q_V + i * KC, 2 + c)
                for m in range(MB):
                    act.wait_ge(pe_chunk, Q_V + (i + 1) * KC)
                    nc.scalar.activation(v[:, m, i * CB:(i + 1) * CB], ps[:, 4 * i + m], ACT.Gelu_apprx_tanh
                                         ).then_inc(v_gelu, 1)
            root(slice(0, NT), NT + 1)
            with act.Fori(0, WB) as i:
                for c in range(3 * KC):
                    hi_at(i, Q_CONV, 3 * KC, 2 + c)
            with act.Fori(0, WB) as i:
                for c in range(KC):
                    hi_at(i, Q_U, KC, 2 + c)
                act.wait_ge(pe_chunk, i * KC + Q_U + KC)
                act.wait_ge(u_used, i + 1)
                for m in range(MB):
                    nc.scalar.activation(sg[:, m], ps[:, m], ACT.Gelu_apprx_tanh).then_inc(u_ready, 1)
            with act.Fori(0, DB) as i:
                for r in range(2):
                    q = r * (KC + WC)
                    for c in range(KC):
                        hi_at(i, Q_MERGE, 2 * (KC + WC), q + 2 + c)
                    act.wait_ge(pe_chunk, i * 2 * (KC + WC) + (Q_MERGE + q + KC))
                    if r == 0:
                        act.wait_ge(u_used, WB + 1)
                        act.wait_ge(mrg_sum, i + 1)
                    else:
                        act.wait_ge(set_free[1], 2 * i + (2 * WB + 2))
                    for m in range(MB):
                        nc.scalar.activation(sg[:, m], ps[:, m], ACT.Sigmoid,
                                             bias=bgate[:, bass.ds(i * MB + r * KT + m, 1)]).then_inc(sg_ready, 1)
                    for c in range(WC):
                        hi_at(i, Q_MERGE, 2 * (KC + WC), q + KC + 2 + c)
            with act.Fori(0, DB - 1) as i:
                for c in range(KC):
                    hi_at(i, Q_OUT, KC, 2 + c)
            for c in range(2, KC):
                hi(Q_OUT + (DB - 1) * KC, c)

            preload(ACT.Sqrt, 2)
            for m in range(NT):
                act.wait_ge(h_ready[1], NT * (DB // 2 - 1) + 1)
                act.wait_ge(h_ready[0], NT * (DB // 2) + 1)
                square(m, h[:, m, 0:D - CB], sumsq, NT + m + 1)
            for m in range(NT):
                act.wait_ge(h_ready[1], NT * (DB // 2 - 1) + m + 2)
                square(m, h[:, m, D - CB:D], sumsq2, 2 * NT + m + 1)
            for m in range(NT):
                root(slice(m, m + 1), NT + 1 + m + 1)
            act.dma_start(rw[:], router_w).then_inc(router_in, 16)
            act.dma_start(rb[:], router_b.partition_broadcast(P).rearrange("p o d -> p (o d)")).then_inc(router_in, 16)
            for m in range(NT):
                for kc in range(KT // 4):
                    t = m * (KT // 4) + kc
                    act.wait_ge(xt_done, t + 1)
                    if m >= 2:
                        act.wait_ge(logit_done, m - 1)
                    nc.scalar.activation(xt[:, m % 2, 4 * kc:4 * kc + 4], ps[:, 4 + t % 4].rearrange("p (k n) -> p k n", k=4),
                                         ACT.Copy).then_inc(xt_ready, 1)
                nc.scalar.activation(xb[:, 0, m], xn[:, m], ACT.Copy).then_inc(xb0_ready, 1)
            preload(ACT.Exp, 3)
            act.wait_ge(gsh_ready, 1)
            nc.scalar.activation(gexp[:], gsh[:], ACT.Exp).then_inc(gexp_ready, 1)
            act.wait_ge(esh_ready, 1)
            nc.scalar.activation(eexp[:], esh[:], ACT.Exp).then_inc(eexp_ready, 1)

            def gathered(u, p):
                for kc in range(KT // 4):
                    act.wait_ge(gat_done, u * (KT // 4) + (kc + 1))
                    nc.scalar.activation(xg[p][:, 4 * kc:4 * kc + 4], ps[:, 6 + kc % 2].rearrange("p (k n) -> p k n", k=4),
                                         ACT.Copy).then_inc(xg_done, 1)

            def silu(u):
                act.wait_ge(used, u * USED + (2 * KX - 1))
                act.wait_ge(h_done, u + 1)
                nc.scalar.activation(sl[:], ps[:, 0], ACT.Silu).then_inc(silu_done, 1)

            def high_y(u):
                for c in range(DX):
                    act.wait_ge(used, u * USED + (2 * KX + c + 1))
                    act.wait_ge(cb_done, u * 4 * NT + (NT * c - NT + 5 if c else 1))
                    nc.scalar.activation(yh[:, c % 2], ps[:, 2 + c % 2], ACT.Copy).then_inc(yh_done, 1)

            def first_products(u):
                act.wait_ge(used, u * USED + 1)

            gathered(0, 0)
            with act.Fori(0, PAIRS // 2 - 1) as w:
                for p in range(2):
                    u = w * 2 + p
                    first_products(u)
                    gathered(u + 1, 1 - p)
                    silu(u)
                    high_y(u)
            first_products(PAIRS - 2)
            gathered(PAIRS - 1, 1)
            silu(PAIRS - 2)
            high_y(PAIRS - 2)
            silu(PAIRS - 1)
            high_y(PAIRS - 1)
            act.wait_ge(table_ready, 1)
            n_over = act.value_load(over_n[0:1, 0:1], min_val=0, max_val=MAX_OVER - 1)
            with act.Fori(0, MAX_OVER - 1) as i:
                with act.If(i < n_over):
                    gathered(i + PAIRS, 0)
                    silu(i + PAIRS)
                    high_y(i + PAIRS)
            act.wait_ge(moe_done, 1)
            for m in range(NT):
                square(m, h[:, m], sumsq, 3 * NT + m + 1)
                root(slice(m, m + 1), 2 * NT + 1 + m + 1)

        @block.tensor
        def _(pe):
            pe.wait_ge(const_in, 16)
            for t in range(NT * KT // 4):
                m, kc = t // (KT // 4), t % (KT // 4)
                pe.wait_ge(xn_ready, m + 1)
                if t >= 4:
                    pe.wait_ge(tr_lo, t - 3)
                for j in range(4):
                    k = 4 * kc + j
                    last = nc.tensor.transpose(ps[:, 4 + t % 4, j * P:(j + 1) * P], xnat[:, m, k * P:(k + 1) * P], ident)
                last.then_inc(tr_done, 1)
            pe.wait_ge(ws_masked, 1)
            pe.wait_ge(sq_done, NT)
            for g in range(G):
                last = nc.tensor.transpose(ps[:, g // 4, (g % 4) * P:(g % 4 + 1) * P], wsraw[:, g], ident)
            last.then_inc(wst_tr, 1)
            pe.wait_ge(wst_ready, 1)
            pe.wait_ge(tr_lo, NT * KT // 4)

            def channel_block(ah, al, kts, base, q):
                for c in range(kts // CK):
                    pe.wait_ge(lo_done, q + c + 1)
                    for j in range(CK):
                        k = c * CK + j
                        for m in range(MB):
                            o = ps[:, base + m]
                            whi = wh[:, c % SPLIT_SLOTS, j, m * P:(m + 1) * P]
                            wlo = wl[:, c % SPLIT_SLOTS, j, m * P:(m + 1) * P]
                            nc.tensor.matmul(o, whi, ah[:, k], start=(k == 0), stop=False)
                            nc.tensor.matmul(o, whi, al[:, k], start=False, stop=False)
                            last = nc.tensor.matmul(o, wlo, ah[:, k], start=False, stop=(k == kts - 1))
                    last.then_inc(pe_chunk, 1)

            def token_block(ah, al, base, q, ready=None):
                for c in range(KC):
                    pe.wait_ge(lo_done, q + c + 1)
                    for j in range(CK):
                        k = c * CK + j
                        if ready is not None:
                            pe.wait_ge(ready, k + 1)
                        for m in range(NT):
                            o = ps[:, base + m]
                            xhi = ah[:, k, m * P:(m + 1) * P]
                            xlo = al[:, k, m * P:(m + 1) * P]
                            nc.tensor.matmul(o, xhi, wh[:, c % SPLIT_SLOTS, j], start=(k == 0), stop=False)
                            nc.tensor.matmul(o, xhi, wl[:, c % SPLIT_SLOTS, j], start=False, stop=False)
                            last = nc.tensor.matmul(o, xlo, wh[:, c % SPLIT_SLOTS, j], start=False, stop=(k == KT - 1))
                    last.then_inc(pe_chunk, 1)

            for i in range(WB):
                token_block(xh, xl, 4 * i, Q_V + i * KC)
            with pe.Fori(0, WB) as i:
                q = i * 3 * KC + Q_CONV
                pe.wait_ge(v_gelu, MB * WB)
                pe.wait_ge(set_free[0], 2 * i + 1)
                channel_block(xh, xl, KT, 0, q)
                pe.wait_ge(set_free[1], i + 1)
                channel_block(xh, xl, KT, 4, q + KC)
                pe.wait_ge(set_free[0], 2 * i + 2)
                channel_block(xh, xl, KT, 0, q + 2 * KC)
            for i in range(WB):
                pe.wait_ge(v_ready, NT)
                pe.wait_ge(set_free[1], WB + i + 1)
                for m in range(MB):
                    g = i * MB + m
                    for n in range(NT):
                        last = nc.tensor.matmul(ps[:, 4 + m, n * P:(n + 1) * P], v[:, n, g * P:(g + 1) * P],
                                                wst[:, g], start=True, stop=True)
                last.then_inc(mixed_done, 1)
                if i == 0:
                    pe.wait_ge(set_free[0], 2 * WB + 1)
                else:
                    pe.wait_ge(u_ready, MB * i)
                channel_block(xh, xl, KT, 0, Q_U + i * KC)
            with pe.Fori(0, DB) as i:
                for r in range(2):
                    q = i * 2 * (KC + WC) + (Q_MERGE + r * (KC + WC))
                    pe.wait_ge(u_ready, MB * WB)
                    pe.wait_ge(sg_ready, i * 2 * MB + (MB * r + 1))
                    channel_block(xh, xl, KT, 0, q)
                    pe.wait_ge(ya_ready if r == 0 else yb_ready, WB)
                    pe.wait_ge(set_free[1], i * 2 + (2 * WB + r + 1))
                    channel_block(yah if r == 0 else ybh, yal if r == 0 else ybl, WT, 4, q + KC)
            with pe.Fori(0, DB // 2) as i:
                for s in range(2):
                    if s == 0:
                        pe.wait_ge(sg_ready, 2 * MB * DB + 1)
                    else:
                        pe.wait_ge(set_free[1], 2 * WB + 2 * DB + 1)
                    pe.wait_ge(h_ready[s], i * NT + 1)
                    token_block(mh, ml, 4 * s, i * 2 * KC + (Q_OUT + s * KC), ready=m_ready)

            for m in range(NT):
                for kc in range(KT // 4):
                    t = m * (KT // 4) + kc
                    pe.wait_ge(xn2_ready, m + 1)
                    if t >= 4:
                        pe.wait_ge(xt_ready, t - 3)
                    else:
                        pe.wait_ge(h_ready[1], NT * (DB // 2) + 1)
                    for j in range(4):
                        k = 4 * kc + j
                        last = nc.tensor.transpose(ps[:, 4 + t % 4, j * P:(j + 1) * P], xn[:, m, k * P:(k + 1) * P], ident)
                    last.then_inc(xt_done, 1)
                pe.wait_ge(router_in, 32)
                pe.wait_ge(sq_done, 3 * NT)
                for k in range(KT):
                    if k % 4 == 0:
                        pe.wait_ge(xt_ready, m * (KT // 4) + k // 4 + 1)
                    last = nc.tensor.matmul(ps[:, m, 0:EG + E], xt[:, m % 2, k], rw[:, k], start=(k == 0), stop=(k == KT - 1))
                last.then_inc(logit_done, 1)

            pe.wait_ge(constb_ready, 1)
            pe.wait_ge(mask_ready, 1)
            pe.wait_ge(xt_ready, NT * KT // 4)
            for n in range(NT):
                for b in range(n + 1):
                    nc.tensor.matmul(ps[:, 4, n * E:(n + 1) * E], before if b == n else ones, m32b[:, b],
                                     start=(b == 0), stop=(b == n))
            nc.tensor.matmul(ps[:, 5, 0:1], m128[:].rearrange("p e t -> p (e t)"), ones[:, 0:1], start=True, stop=True
                             ).then_inc(rank_done, 1)
            pe.wait_ge(active_ready, 1)
            nc.tensor.matmul(ps[:, 5, 2:3], before, activeb[:], start=True, stop=True).then_inc(prefix_done, 1)
            pe.wait_ge(unit_ready, 1)
            for k, t in enumerate((cand_e, cand_r, ones)):
                last = nc.tensor.matmul(ps[:, 6, k * MAX_OVER:(k + 1) * MAX_OVER], t, unit_ohb[:], start=True, stop=True)
            last.then_inc(table_done, 1)

            HALF = (slice(0, CAP), slice(CAP, 2 * CAP))

            def gather(u, first, last_kc):
                for kc in range(first, last_kc):
                    pe.wait_ge(sel_ready, u + 1)
                    pe.wait_ge(xg_done, u * (KT // 4) + (kc + 1))
                    for j in range(4):
                        k = 4 * kc + j
                        for n in range(NT):
                            for b in range(3):
                                last = nc.tensor.matmul(ps[:, 6 + kc % 2, j * P:(j + 1) * P], xb[:, b, n, k * P:(k + 1) * P],
                                                        selb[:, n], start=(n == 0 and b == 0), stop=(n == NT - 1 and b == 2))
                    last.then_inc(gat_done, 1)

            def added(u):
                pe.wait_ge(add_done, u * (DX * NT) + NT)

            def turn_selection(u):
                added(u)
                pe.wait_ge(xg_done, (u + 1) * (KT // 4) + 2)
                for n in range(NT):
                    nc.tensor.transpose(ps[:, 6, n * P:(n + 1) * P], self_[:, n], ident)
                for n in range(NT):
                    last = nc.tensor.matmul(ps[:, 7, 0:2], self_[:, n], wc[:, n], start=(n == 0), stop=(n == NT - 1))
                last.then_inc(seltr_done, 1)

            def landed(u, c):
                pe.wait_ge(ring_in[c % RING], u * (2 * LX // RING * 16) + (c // RING + 1) * 16)

            def gate_up(u, p, l, pair=True):
                landed(u, 2 * l)
                if pair:
                    landed(u, 2 * l + 1)
                kc = l // 2
                for j in range(EK):
                    first, end = kc == 0 and j == 0, kc == KX - 1 and j == EK - 1
                    if pair:
                        for ab in range(2):
                            last = nc.tensor.matmul(ps[HALF[ab], l % 2], xg[p][:, EK * kc + j, HALF[ab]],
                                                    ring[(2 * l + ab) % RING][:, j], start=first, stop=end,
                                                    skip_group_check=True)
                    else:
                        last = nc.tensor.matmul(ps[:, l % 2], xg[p][:, EK * kc + j], ring[2 * l % RING][:, j],
                                                start=first, stop=end)
                last.then_inc(used, 1)

            def turn_hidden(u):
                pe.wait_ge(h_done, u + 2)
                for j in range(EK):
                    last = nc.tensor.transpose(ps[:, 0, j * P:(j + 1) * P], hh[:, j * P:(j + 1) * P], ident)
                last.then_inc(htr_done, 1)
                pe.wait_ge(ht_ready, u + 1)

            def down(u, c, pair=True):
                l = 2 * KX + c
                landed(u, 2 * l)
                if pair:
                    landed(u, 2 * l + 1)
                pe.wait_ge(y_split, u * DX + (c + 1))
                for j in range(EK):
                    if pair:
                        for ab in range(2):
                            last = nc.tensor.matmul(ps[HALF[ab], 2 + c % 2], ht[:, j, HALF[ab]], ring[(2 * l + ab) % RING][:, j],
                                                    start=(j == 0), stop=(j == EK - 1), skip_group_check=True)
                    else:
                        last = nc.tensor.matmul(ps[:, 2 + c % 2], ht[:, j], ring[2 * l % RING][:, j],
                                                start=(j == 0), stop=(j == EK - 1))
                last.then_inc(used, 1)

            def combine(u, c):
                pe.wait_ge(y_split, u * DX + (c + 3))
                for n in range(NT):
                    pe.wait_ge(add_done, u * (DX * NT) + (c * NT + n + 1))
                    nc.tensor.matmul(ps[:, 4 + n], selt[:, n], yh[:, c % 2], start=True, stop=False)
                    nc.tensor.matmul(ps[:, 4 + n], selt[:, n], yl[:, c % 2], start=False, stop=True).then_inc(cb_done, 1)

            def back(u, gathered, pair=True):
                pe.wait_ge(selt_done, u + 1)
                down(u, 0, pair)
                pe.wait_ge(xg_done, gathered * (KT // 4) + 2)
                for c in range(1, DX):
                    down(u, c, pair)
                    combine(u, c - 1)
                combine(u, DX - 1)

            def pair_unit(u, p, more):
                gate_up(u, p, 0)
                turn_selection(u)
                gate_up(u, p, 1)
                for l in range(2, 2 * KX):
                    gate_up(u, p, l)
                    if more and l < 2 + KT // 4:
                        pe.wait_ge(selt_done, u + 1)
                        gather(u + 1, l - 2, l - 1)
                turn_hidden(u)
                back(u, u + 2 if more else u + 1)

            pe.wait_ge(xb0_ready, NT)
            pe.wait_ge(xb1_ready, NT)
            pe.wait_ge(xb2_ready, NT)
            pe.wait_ge(table_ready, 1)
            gather(0, 0, KT // 4)
            with pe.Fori(0, PAIRS // 2 - 1) as w:
                for p in range(2):
                    pair_unit(w * 2 + p, p, more=True)
            pair_unit(PAIRS - 2, 0, more=True)
            pair_unit(PAIRS - 1, 1, more=False)
            n_over = pe.value_load(over_n[0:1, 0:1], min_val=0, max_val=MAX_OVER - 1)
            with pe.Fori(0, MAX_OVER - 1) as i:
                with pe.If(i < n_over):
                    u = i + PAIRS
                    added(u)
                    gather(u, 0, KT // 4)
                    turn_selection(u)
                    for l in range(2 * KX):
                        gate_up(u, 0, l, pair=False)
                    turn_hidden(u)
                    back(u, u + 1, pair=False)

        @block.vector
        def _(dve):
            for s, credit in CREDITS:
                dve.sem_inc(s, credit)
            nc.vector.memset(warm[:], 1.0).then_inc(warm_ready, 1)
            step = [0]

            def link(ins):
                step[0] += 1
                ins.then_inc(dve_step, 1)
                dve.wait_ge(dve_step, step[0])

            def finish_root(m, n, link=link):
                nc.vector.reciprocal(rvar[:, m], var[:, m]).then_inc(rvar_ready, 1)
                dve.wait_ge(root_done, n)
                link(nc.vector.tensor_tensor(rvar[:, m], rstd[:, m], rstd[:, m], ALU.mult))
                link(nc.vector.tensor_tensor(rvar[:, m], rvar[:, m], var[:, m], ALU.mult))
                link(nc.vector.tensor_scalar(rvar[:, m], rvar[:, m], -0.5, 1.5, ALU.mult, ALU.add))
                link(nc.vector.tensor_tensor(rstd[:, m], rstd[:, m], rvar[:, m], ALU.mult))

            def norm(m, squares_done, n, link=link):
                m = slice(m, m + 1)
                dve.wait_ge(sq_done, squares_done)
                link(nc.vector.tensor_scalar(var[:, m], sumsq[:, m], 1.0 / D, EPS, ALU.mult, ALU.add))
                finish_root(m, n, link)

            def turned_low(m):
                for kc in range(KT // 4):
                    t = m * (KT // 4) + kc
                    dve.wait_ge(tr_hi, t + 1)
                    dst = slice(4 * kc, 4 * kc + 4), slice(m * P, (m + 1) * P)
                    nc.vector.tensor_tensor(xl[:, dst[0], dst[1]], ps[:, 4 + t % 4].rearrange("p (k n) -> p k n", k=4),
                                            xh[:, dst[0], dst[1]].bitcast(F32), ALU.subtract).then_inc(tr_lo, 1)

            dve.wait_ge(const_in, 16)
            nc.vector.tensor_copy(constb[:].rearrange("p a b -> p (a b)"), wide).then_inc(constb_ready, 1)
            for m in range(NT):
                norm(m, m + 1, m + 1)
                dve.wait_ge(g1_in, 16)
                nc.vector.scalar_tensor_tensor(out=xnat[:, m], in0=xnat[:, m], scalar=rstd[:, m:m + 1], in1=g1bc[:],
                                               op0=ALU.mult, op1=ALU.mult).then_inc(xn_ready, 1)
                if m >= 1:
                    turned_low(m - 1)
            turned_low(NT - 1)
            dve.wait_ge(wst_tr, 1)
            nc.vector.tensor_copy(wst[:].rearrange("p g t -> p (g t)"), ps[:, 0:2].rearrange("p a b -> p (a b)")
                                  ).then_inc(wst_ready, 1)

            for m in range(NT):
                dve.wait_ge(v_gelu, NT * (WB - 1) + m + 1)
                for b in range(WB):
                    last = nc.vector.bn_stats(bnst[:, m, b], v[:, m, b * CB:(b + 1) * CB])
                link(last)
                link(nc.vector.bn_aggr(bnag[:, m], bnst[:, m].rearrange("p a b -> p (a b)")))
            link(nc.vector.tensor_scalar(var[:], bnag[:, :, 1:2].rearrange("p m o -> p (m o)"), EPS, None, ALU.add))
            finish_root(slice(0, NT), NT + 1)
            dve.wait_ge(small_in, 16 * N_SMALL)
            for m in range(NT):
                link(nc.vector.tensor_scalar(v[:, m], v[:, m], bnag[:, m, 0:1], rstd[:, m:m + 1], ALU.subtract, ALU.mult))
                link(nc.vector.tensor_tensor(v[:, m], v[:, m], lng[:], ALU.mult))
                nc.vector.tensor_tensor(v[:, m], v[:, m], lnb[:], ALU.add).then_inc(v_ready, 1)
            nc.vector.memset(xc[:, :, 0:2], 0.0).then_inc(pad_zero, 1)

            def chain_in(i, per, base):
                local = [0]

                def chain(ins):
                    local[0] += 1
                    ins.then_inc(dve_step, 1)
                    dve.wait_ge(dve_step, i * per + (base + local[0]))
                return chain

            CONV_STEPS = 4
            with dve.Fori(0, WB) as i:
                chain = chain_in(i, CONV_STEPS, step[0])
                q = i * 3 * KC + Q_CONV
                dve.wait_ge(pe_chunk, q + KC)
                for m in range(MB):
                    last = nc.vector.tensor_copy(cbuf[:, m], ps[:, m])
                last.then_inc(set_free[0], 1)
                dve.wait_ge(set_free[0], 2 * i + 2)
                dve.wait_ge(pe_chunk, q + 2 * KC)
                dve.wait_ge(pad_zero, 1)
                for m in range(MB):
                    last = nc.vector.tensor_tensor(xc[:, m, 2:N + 2], ps[:, 4 + m], cbuf[:, m], ALU.mult)
                last.then_inc(set_free[1], 1)
                dve.wait_ge(set_free[1], i + 2)
                for k in (2, 1, 0):
                    for m in range(MB):
                        w = convw[:, k, bass.ds(i * MB + m, 1)]
                        if k == 2:
                            last = nc.vector.tensor_scalar(cbuf[:, m], xc[:, m, 2:N + 2], w, None, ALU.mult)
                        else:
                            last = nc.vector.scalar_tensor_tensor(out=cbuf[:, m], in0=xc[:, m, k:k + N], scalar=w,
                                                                  in1=cbuf[:, m], op0=ALU.mult, op1=ALU.add)
                    chain(last)
                dve.wait_ge(pe_chunk, q + 3 * KC)
                for m in range(MB):
                    last = nc.vector.tensor_tensor(cbuf[:, m], ps[:, m], cbuf[:, m], ALU.mult)
                last.then_inc(set_free[0], 1)
                dve.wait_ge(set_free[0], 2 * i + 3)
                mine = bass.ds(i * MB, MB)
                chain(nc.vector.tensor_copy(yah[:, mine], cbuf[:]))
                nc.vector.tensor_tensor(yal[:, mine], cbuf[:], yah[:, mine].bitcast(F32), ALU.subtract
                                        ).then_inc(ya_ready, 1)
                dve.wait_ge(ya_ready, i + 1)
            step[0] += WB * CONV_STEPS

            SGU_STEPS = 1
            with dve.Fori(0, WB) as i:
                chain = chain_in(i, SGU_STEPS, step[0])
                dve.wait_ge(mixed_done, i + 1)
                for m in range(MB):
                    bias = sgub[:, bass.ds(i * MB + m, 1)].to_broadcast([P, NT, P])
                    last = nc.vector.tensor_tensor(mx[:, m].rearrange("p (n t) -> p n t", n=NT),
                                                   ps[:, 4 + m].rearrange("p (n t) -> p n t", n=NT), bias, ALU.add)
                last.then_inc(set_free[1], 1)
                dve.wait_ge(set_free[1], i + (WB + 2))
                dve.wait_ge(u_ready, MB * i + MB)
                nc.vector.tensor_tensor(mx[:], mx[:], sg[:], ALU.mult).then_inc(u_used, 1)
                dve.wait_ge(u_used, i + 2)
                mine = bass.ds(i * MB, MB)
                chain(nc.vector.tensor_copy(ybh[:, mine], mx[:]))
                nc.vector.tensor_tensor(ybl[:, mine], mx[:], ybh[:, mine].bitcast(F32), ALU.subtract
                                        ).then_inc(yb_ready, 1)
                dve.wait_ge(yb_ready, i + 1)
            step[0] += WB * SGU_STEPS

            def merge(i, r):
                mine = bass.ds(i * MB, MB)
                dve.wait_ge(pe_chunk, i * 2 * (KC + WC) + (Q_MERGE + (r + 1) * (KC + WC)))
                dve.wait_ge(sg_ready, i * 2 * MB + (MB * (r + 1) + 1))
                if r == 0:
                    nc.vector.tensor_tensor(mrg[:, mine], ps[:, 4:8], sg[:], ALU.mult).then_inc(set_free[1], 1)
                else:
                    nc.vector.tensor_tensor(sg[:], ps[:, 4:8], sg[:], ALU.mult).then_inc(set_free[1], 1)
                    dve.wait_ge(set_free[1], i * 2 + (2 * WB + 3))
                    nc.vector.tensor_tensor(mrg[:, mine], mrg[:, mine], sg[:], ALU.add).then_inc(mrg_sum, 1)
                    dve.wait_ge(mrg_sum, i + 2)

            def split_merged(first, last):
                for k in range(first, last):
                    link(nc.vector.tensor_copy(mh[:, k], mrg[:, k]))
                    nc.vector.tensor_tensor(ml[:, k], mrg[:, k], mh[:, k].bitcast(F32), ALU.subtract).then_inc(m_ready, 1)

            with dve.Fori(0, DB - 1) as i:
                for r in range(2):
                    merge(i, r)
            merge(DB - 1, 0)
            dve.wait_ge(pe_chunk, Q_OUT - WC)
            split_merged(0, KT - MB)
            merge(DB - 1, 1)
            split_merged(KT - MB, KT)
            dve.wait_ge(h_in, 16 * NT)
            with dve.Fori(0, DB // 2) as i:
                for s in range(2):
                    dve.wait_ge(pe_chunk, i * 2 * KC + (Q_OUT + (s + 1) * KC))
                    for m in range(NT):
                        hs = h[:, m, bass.ds(i * 2 * CB + s * CB, CB)]
                        nc.vector.tensor_tensor(hs, hs, ps[:, 4 * s + m], ALU.add).then_inc(h_ready[s], 1)

            dve.wait_ge(g2_in, 16)
            for m in range(NT):
                dve.wait_ge(sq_done, 2 * NT + m + 1)
                link(nc.vector.tensor_tensor(sumsq[:, m:m + 1], sumsq[:, m:m + 1], sumsq2[:, m:m + 1], ALU.add))
                norm(m, 2 * NT + m + 1, NT + 1 + m + 1)
                nc.vector.scalar_tensor_tensor(out=xn[:, m], in0=h[:, m], scalar=rstd[:, m:m + 1], in1=g2bc[:],
                                               op0=ALU.mult, op1=ALU.mult).then_inc(xn2_ready, 1)
            for m in range(NT):
                dve.wait_ge(xb0_ready, m + 1)
                dve.wait_ge(xt_done, (m + 1) * (KT // 4))
                nc.vector.tensor_tensor(xn[:, m], xn[:, m], xb[:, 0, m], ALU.subtract).then_inc(xr_done, 1)
                dve.wait_ge(xr_done, m + 1)
                nc.vector.tensor_copy(xb[:, 1, m], xn[:, m]).then_inc(xb1_ready, 1)
            dve.wait_ge(router_in, 32)
            dve.wait_ge(logit_done, NT)
            for m in range(NT):
                last = nc.vector.tensor_tensor(lg[:, m], ps[:, m, 0:EG + E], rb[:], ALU.add)
            link(last)

            def wide_n(ap, k):
                return ap.to_broadcast([P, NT, k])

            def top(dst, code, best):
                link(nc.vector.tensor_reduce(best[:], code[:], AX, ALU.max))
                link(nc.vector.tensor_tensor(dst[:], code[:], wide_n(best[:], code.shape[2]), ALU.is_equal))

            gl = lg[:, :, 0:EG]
            link(nc.vector.tensor_reduce(gmax[:], gl, AX, ALU.max))
            nc.vector.tensor_tensor(gsh[:], gl, wide_n(gmax[:], EG), ALU.subtract).then_inc(gsh_ready, 1)
            dve.wait_ge(gsh_ready, 1)
            link(nc.vector.scalar_tensor_tensor(out=gcode[:], in0=gsh[:], scalar=0.0, in1=desc_g.unsqueeze(1).to_broadcast([P, NT, EG]),
                                                op0=ALU.is_ge, op1=ALU.mult))
            top(goh, gcode, gtop)
            link(nc.vector.tensor_tensor(emask[:], lg[:, :, EG:].rearrange("p n (g e) -> p n g e", g=EG),
                                         goh[:].unsqueeze(3).to_broadcast([P, NT, EG, EPG]), ALU.mult))
            link(nc.vector.tensor_reduce(esel[:], emask[:].rearrange("p n g e -> p n e g"), AX, ALU.add))
            link(nc.vector.tensor_reduce(emax[:], esel[:], AX, ALU.max))
            nc.vector.tensor_tensor(esh[:], esel[:], wide_n(emax[:], EPG), ALU.subtract).then_inc(esh_ready, 1)
            dve.wait_ge(esh_ready, 1)
            de = desc_e.unsqueeze(1).to_broadcast([P, NT, EPG])
            link(nc.vector.scalar_tensor_tensor(out=ecode[:], in0=esh[:], scalar=0.0, in1=de, op0=ALU.is_ge, op1=ALU.mult))
            top(oh1, ecode, etop)
            link(nc.vector.scalar_tensor_tensor(out=es2[:], in0=oh1[:], scalar=-3.0e38, in1=esh[:], op0=ALU.mult, op1=ALU.add))
            link(nc.vector.tensor_reduce(emax[:], es2[:], AX, ALU.max))
            link(nc.vector.tensor_tensor(ecode[:], es2[:], wide_n(emax[:], EPG), ALU.is_equal))
            link(nc.vector.tensor_tensor(ecode[:], ecode[:], de, ALU.mult))
            top(oh2, ecode, etop)
            link(nc.vector.tensor_tensor(m8[:], oh1[:], oh2[:], ALU.add))
            dve.wait_ge(gexp_ready, 1)
            link(nc.vector.tensor_reduce(gsum[:], gexp[:], AX, ALU.add))
            link(nc.vector.reciprocal(gw[:], gsum[:]))
            dve.wait_ge(eexp_ready, 1)
            link(nc.vector.tensor_tensor(p8[:], eexp[:], m8[:], ALU.mult))
            link(nc.vector.tensor_reduce(den[:], p8[:], AX, ALU.add))
            link(nc.vector.reciprocal(rden[:], den[:]))
            link(nc.vector.tensor_tensor(rden[:], rden[:], gw[:], ALU.mult))
            link(nc.vector.tensor_tensor(p8[:], p8[:], wide_n(rden[:], EPG), ALU.mult))
            g4 = goh[:].unsqueeze(3).to_broadcast([P, NT, EG, EPG])
            link(nc.vector.tensor_tensor(w32[:].rearrange("p n (g e) -> p n g e", g=EG), g4,
                                         p8[:].unsqueeze(2).to_broadcast([P, NT, EG, EPG]), ALU.mult))
            link(nc.vector.tensor_tensor(m32[:], g4, m8[:].unsqueeze(2).to_broadcast([P, NT, EG, EPG]), ALU.mult))
            nc.vector.tensor_copy(m32b[:], m32[:].rearrange("p n g e -> p n (g e)"))
            link(nc.vector.tensor_reduce(msum[:], m32[:].rearrange("p n g e -> p (g e) n"), AX, ALU.add))
            nc.vector.tensor_copy(m128[:], msum[:].unsqueeze(2).to_broadcast([P, E, P // E])).then_inc(mask_ready, 1)

            dve.wait_ge(rank_done, 1)
            link(nc.vector.scalar_tensor_tensor(out=pos[:].rearrange("p n e -> p (n e)"), in0=ps[:, 4, 0:NT * E], scalar=1.0,
                                                in1=m32[:].rearrange("p n g e -> p (n g e)"), op0=ALU.add, op1=ALU.mult))
            link(nc.vector.tensor_scalar(pos[:], pos[:], -1.0, None, ALU.add))
            link(nc.vector.tensor_tensor(active[:], ps[:, 5, 0:1], const[:, 4 * P:4 * P + 1], ALU.is_gt))
            nc.vector.tensor_copy(activeb[:], active[:]).then_inc(active_ready, 1)
            dve.wait_ge(prefix_done, 1)
            link(nc.vector.tensor_copy(prefix[:], ps[:, 5, 2:3]))
            link(nc.vector.tensor_scalar(unit_oh[:], iota_u, prefix[:], active[:], ALU.is_equal, ALU.mult))
            nc.vector.tensor_copy(unit_ohb[:], unit_oh[:]).then_inc(unit_ready, 1)
            dve.wait_ge(table_done, 1)
            nc.vector.tensor_copy(over_e[:], ps[0:1, 6, 0:MAX_OVER])
            nc.vector.tensor_copy(over_r[:], ps[:, 6, MAX_OVER:2 * MAX_OVER])
            link(nc.vector.tensor_reduce(over_nf[:], ps[:, 6, 2 * MAX_OVER:3 * MAX_OVER], AX, ALU.add))
            nc.vector.tensor_copy(over_n[:], over_nf[0:1]).then_inc(table_ready, 1)
            dve.wait_ge(table_ready, 1)

            def select(link_):
                link_(nc.vector.tensor_tensor(self_[:].rearrange("p n (h c) -> p n h c", h=2),
                                              iota_c.unsqueeze(1).unsqueeze(1).to_broadcast([P, NT, 2, CAP]),
                                              pc[:].unsqueeze(3).to_broadcast([P, NT, 2, CAP]), ALU.is_equal))
                nc.vector.tensor_copy(selb[:], self_[:]).then_inc(sel_ready, 1)

            def take_selection(u):
                dve.wait_ge(seltr_done, u + 1)
                nc.vector.tensor_copy(selt[:].rearrange("p n t -> p (n t)"), ps[:, 6])
                nc.vector.tensor_copy(wsl[0:CAP], ps[0:CAP, 7, 0:1])
                nc.vector.tensor_copy(wsl[CAP:], ps[CAP:, 7, 1:2]).then_inc(selt_done, 1)

            def hidden(u):
                dve.wait_ge(silu_done, u + 1)
                dve.wait_ge(used, u * USED + 2 * KX)
                dve.wait_ge(selt_done, u + 1)
                nc.vector.scalar_tensor_tensor(out=hh[:], in0=ps[:, 1], scalar=wsl[:], in1=sl[:], op0=ALU.mult,
                                               op1=ALU.mult).then_inc(h_done, 1)

            def take_hidden(u):
                dve.wait_ge(htr_done, u + 1)
                nc.vector.tensor_copy(ht[:].rearrange("p j s -> p (j s)"), ps[:, 0]).then_inc(ht_ready, 1)

            def low_y(u, c):
                dve.wait_ge(yh_done, u * DX + (c + 1))
                nc.vector.tensor_tensor(yl[:, c % 2], ps[:, 2 + c % 2], yh[:, c % 2].bitcast(F32), ALU.subtract
                                        ).then_inc(y_split, 1)

            def add(u, c):
                for n in range(NT):
                    dve.wait_ge(cb_done, u * (DX * NT) + (c * NT + n + 6))
                    hs = h[:, n, c * CB:(c + 1) * CB]
                    nc.vector.tensor_tensor(hs, hs, ps[:, 4 + n], ALU.add).then_inc(add_done, 1)

            def back(u):
                hidden(u)
                take_hidden(u)
                low_y(u, 0)
                for c in range(1, DX):
                    low_y(u, c)
                    add(u, c - 1)
                add(u, DX - 1)

            dve.wait_ge(xb2_ready, NT)
            nc.vector.tensor_copy(pc[:], pos[:, :, 0:2])
            link(nc.vector.tensor_copy(wc[:], w32[:, :, 0:2]))
            select(link)
            SEL_STEPS = 2
            with dve.Fori(0, PAIRS - 1) as u:
                chain = chain_in(u, SEL_STEPS, step[0])
                take_selection(u)
                nc.vector.tensor_copy(pc[:], pos[:, :, bass.ds(u * 2 + 2, 2)])
                chain(nc.vector.tensor_copy(wc[:], w32[:, :, bass.ds(u * 2 + 2, 2)]))
                select(chain)
                back(u)
            step[0] += (PAIRS - 1) * SEL_STEPS

            def select_over(i, chain):
                e = dve.value_load(over_e[0:1, bass.ds(i, 1)], min_val=0, max_val=E - 1)
                for n in range(NT):
                    nc.vector.tensor_scalar(wc[:, n], w32[:, n, bass.ds(e, 1)].to_broadcast([P, 2]), 0.0, None, ALU.add)
                    last = nc.vector.tensor_scalar(pc[:, n, 0:1], pos[:, n, bass.ds(e, 1)],
                                                   over_r[:, bass.ds(i, 1)], None, ALU.subtract)
                chain(last)
                chain(nc.vector.tensor_scalar(pc[:, :, 1:2], pc[:, :, 0:1], -float(CAP), None, ALU.add))
                select(chain)

            take_selection(PAIRS - 1)
            select_over(0, link)
            back(PAIRS - 1)
            n_over = dve.value_load(over_n[0:1, 0:1], min_val=0, max_val=MAX_OVER - 1)
            OVER_STEPS = 3
            with dve.Fori(0, MAX_OVER - 1) as i:
                with dve.If(i < n_over):
                    u = i + PAIRS
                    take_selection(u)
                    select_over(i + 1, chain_in(i, OVER_STEPS, step[0]))
                    back(u)
            dve.wait_ge(add_done, n_over * (DX * NT) + (PAIRS * DX * NT + NT))
            nc.vector.memset(prefix[:], 0.0).then_inc(moe_done, 1)
            step_end = sem("step_end")
            dve.wait_ge(fg_in, 16)
            end_steps = [0]

            def end_link(ins):
                end_steps[0] += 1
                ins.then_inc(step_end, 1)
                dve.wait_ge(step_end, end_steps[0])

            for m in range(NT):
                norm(m, 3 * NT + m + 1, 2 * NT + 1 + m + 1, end_link)
                nc.vector.scalar_tensor_tensor(out=h[:, m], in0=h[:, m], scalar=rstd[:, m:m + 1], in1=fgbc[:],
                                               op0=ALU.mult, op1=ALU.mult).then_inc(out_ready, 1)


def mixer_stream(w_in, w_branch, w_out):
    import numpy as np
    D, W = w_in.shape[0], w_branch.shape[1]
    blocks = []
    for i in range(W // CB):
        blocks.append((w_in, 4 * W + i * CB))
    for i in range(W // CB):
        blocks += [(w_in, b * W + i * CB) for b in (0, 2, 1)]
    for i in range(W // CB):
        blocks.append((w_in, 3 * W + i * CB))
    for i in range(D // CB):
        for r in range(w_branch.shape[0]):
            blocks += [(w_in, 5 * W + r * D + i * CB), (w_branch[r], i * CB)]
    for i in range(D // CB):
        blocks.append((w_out, i * CB))
    rows = CK * P
    stream = np.empty((sum(w.shape[0] // rows for w, _ in blocks), P, CK * CB), w_in.dtype)
    q = 0
    for w, col in blocks:
        n = w.shape[0] // rows
        stream[q:q + n].reshape(n, P, CK, CB)[:] = w[:, col:col + CB].reshape(n, CK, P, CB).transpose(0, 2, 1, 3)
        q += n
    return stream


def expert_stream(w_gate, w_up, w_down):
    import numpy as np
    E, D, F = w_gate.shape
    KC, DC = D // (EK * P), D // CB
    stream = np.empty((E, 2 * KC + DC, P, EK, CB), w_gate.dtype)
    stream[:, 0:2 * KC:2] = w_gate.reshape(E, KC, EK, P, F).transpose(0, 1, 3, 2, 4)
    stream[:, 1:2 * KC:2] = w_up.reshape(E, KC, EK, P, F).transpose(0, 1, 3, 2, 4)
    stream[:, 2 * KC:] = w_down.reshape(E, EK, P, DC, CB).transpose(0, 3, 2, 1, 4)
    return stream.reshape(E * (2 * KC + DC), P, EK * CB)


def shape_constants(EG, E):
    import numpy as np
    c = np.arange(P)
    per = P // E
    parts = [np.eye(P), c[:, None] < c[None, :], np.ones((P, P)),
             np.repeat(c[:, None] // per, P, axis=1),
             np.repeat(CAP + 2 * CAP * (c[:, None] % per), P, axis=1),
             np.tile(np.arange(CAP), (P, 1)), np.tile(np.arange(MAX_OVER), (P, 1)),
             np.tile(np.arange(EG, 0, -1), (P, 1)), np.tile(np.arange(E // EG, 0, -1), (P, 1))]
    return np.concatenate(parts, axis=1).astype(np.float32)


def kernel(x, norm1_g, w_in, b_gate, conv_w, ln_v_g, ln_v_b, sgu_w, sgu_b, w_branch, w_out,
           norm2_g, router_g, router_g_b, router_e, router_e_b, w_gate, w_up, w_down, final_g):
    import numpy as _np
    import concourse.bacc as _bacc
    from concourse import mybir as _mybir
    from concourse.bass_utils import run_bass_kernel_spmd as _run

    assert w_in.shape[0] == 1
    D = x.shape[2]
    laid = {
        'x': x,
        'norm1_g': norm1_g,
        'mixer_w': mixer_stream(w_in[0], w_branch[0], w_out[0]),
        'b_gate': b_gate[0].reshape(-1, P).T,
        'conv_w': conv_w[0].reshape(conv_w.shape[1], -1, P).transpose(2, 0, 1),
        'ln_v_g': ln_v_g, 'ln_v_b': ln_v_b, 'sgu_w': sgu_w, 'sgu_b': sgu_b,
        'norm2_g': norm2_g,
        'router_w': _np.concatenate([router_g[0], router_e[0]], axis=1).reshape(D // P, P, -1).transpose(1, 0, 2),
        'router_b': _np.concatenate([router_g_b, router_e_b], axis=1),
        'expert_w': expert_stream(w_gate[0], w_up[0], w_down[0]),
        'final_g': final_g.reshape(1, -1),
        'consts': shape_constants(router_g.shape[2], router_e.shape[2]),
    }
    nc = _bacc.Bacc("TRN2", target_bir_lowering=False, num_devices=1)
    arrays, args = {}, []
    for name, a in laid.items():
        a = _np.ascontiguousarray(a)
        arrays[f"in_{name}_dram"] = a
        args.append(nc.dram_tensor(f"in_{name}_dram", a.shape, _mybir.dt.from_np(a.dtype), kind="ExternalInput").ap())
    args.append(nc.dram_tensor("out_0_dram", x.shape, _mybir.dt.from_np(_np.dtype('float32')), kind="ExternalOutput").ap())
    hybrid_block(nc, *args)
    r = _run(nc, [arrays], core_ids=[0])
    return r.results[0]["out_0_dram"]
```

```python
from contextlib import ExitStack

import concourse.bass as bass
from concourse import mybir

P = 128
F32 = mybir.dt.float32
F32R = mybir.dt.float32r
BF16 = mybir.dt.bfloat16
I32 = mybir.dt.int32
ALU = mybir.AluOpType
ACT = mybir.ActivationFunctionType
AX = mybir.AxisListType.X

EPS = 1e-6
CB = 512
CK = 2
RAW_SLOTS = 4
SPLIT_SLOTS = 2
EK = 4
TILE = 32
CAP = 2 * TILE
MAX_OVER = 16
RING = 8


def hybrid_block(nc, x, norm1_g, mixer_w, b_gate, conv_w, ln_v_g, ln_v_b, sgu_w, sgu_b,
                 norm2_g, router_w, router_b, expert_w, final_g, consts, out):
    _, N, D = x.shape
    W = ln_v_g.shape[1]
    G = sgu_w.shape[1]
    KT, NT, WT = D // P, N // P, W // P
    KC, WC = KT // CK, WT // CK
    DB, WB = D // CB, W // CB
    MB = CB // P
    assert NT == 4 and MB == 4 and sgu_w.shape[2] == P

    EG = 4
    E = router_w.shape[2] - EG
    EPG = E // EG
    PAIRS = E // 2
    PER = P // E
    assert TILE + PER * P >= N and 2 * N // (CAP + 1) < MAX_OVER and 4 * TILE == P
    KX = D // (EK * P)
    DX = D // CB
    LX = 2 * KX + DX
    USED = LX
    assert 2 * LX % RING == 0 and EK * P == CB and MB == EK

    x_v = x[0].rearrange("(m p) d -> p m d", p=P)
    out_v = out[0].rearrange("(m p) d -> p m d", p=P)

    Q_V = 0
    Q_CONV = Q_V + WB * KC
    Q_U = Q_CONV + WB * 3 * KC
    Q_MERGE = Q_U + WB * KC
    Q_OUT = Q_MERGE + DB * 2 * (KC + WC)
    Q_END = Q_OUT + DB * KC

    with ExitStack() as ctx:
        def sb(name, shape, dt=F32):
            return ctx.enter_context(nc.sbuf_tensor(name, shape, dt))

        def sem(name):
            return ctx.enter_context(nc.semaphore(name))

        const = sb("const", [P, consts.shape[1]])
        ident = const[:, 0:P]
        place = [4 * P]

        def const_part(n):
            place[0] += n
            return const[:, place[0] - n:place[0]]

        iota_c, iota_u, desc_g, desc_e, key_row, key_col, cand_t = (
            const_part(n) for n in (E, MAX_OVER, EG, EPG, E, 1, 1))
        wide = const[:, P:4 * P]
        constb = sb("constb", [P, 3, P], BF16)
        before, ones, cand_e = (constb[:, k] for k in range(3))
        pos = sb("pos", [P, NT, E])
        w32 = sb("w32", [P, NT, E])
        pc, wc = sb("pc", [P, NT, 4]), sb("wc", [P, NT, 3])
        order, shared_e = sb("order", [1, E], I32), sb("shared_e", [1, PAIRS], I32)
        shared_b, shared_r = sb("shared_b", [1, PAIRS], I32), sb("shared_r", [P, PAIRS])
        wsl = sb("wsl", [P, 1])
        over_n, over_e = sb("over_n", [1, 1], I32), sb("over_e", [1, MAX_OVER], I32)
        over_r = sb("over_r", [P, MAX_OVER])
        bgate = sb("bgate", [P, 2 * KT])
        convw = sb("convw", [P, 3, WT])
        sumsq, sumsq2 = sb("sumsq", [P, NT]), sb("sumsq2", [P, NT])
        warm = sb("warm", [P, 4])
        rstd = sb("rstd", [P, NT])
        var = sb("var", [P, NT])
        rvar = sb("rvar", [P, NT])
        bnst = sb("bnst", [P, NT, 2, 6])
        bnag = sb("bnag", [P, NT, 2])

        BASE = 24544
        assert nc.sbuf_base <= BASE, nc.sbuf_base

        def at(name, shape, dt, kib):
            return nc.alloc_sbuf_tensor_at(name, shape, dt, offset=BASE + int(kib * 1024))

        xh, xl = at("xh", [P, KT, N], F32R, 0), at("xl", [P, KT, N], F32R, 32)
        mh, ml = at("mh", [P, KT, N], F32R, 0), at("ml", [P, KT, N], F32R, 32)
        yah, yal = at("yah", [P, WT, N], F32R, 64), at("yal", [P, WT, N], F32R, 80)
        ybh, ybl = at("ybh", [P, WT, N], F32R, 96), at("ybl", [P, WT, N], F32R, 112)
        xnat = at("xnat", [P, NT, D], F32, 64)
        g1bc = at("g1bc", [P, D], F32, 96)
        wsraw = at("wsraw", [P, G, P], F32, 104)
        cbuf = at("cbuf", [P, MB, N], F32, 96)
        xc = at("xc", [P, MB, N + 2], F32, 104)
        lng, lnb = at("lng", [P, W], F32, 116), at("lnb", [P, W], F32, 120)
        h = at("h", [P, NT, D], F32, 64)
        v = at("v", [P, NT, W], F32, 128)
        wst = at("wst", [P, G, P], F32, 144)
        sgub = at("sgub", [P, G, P], F32, 148)
        mx = at("mx", [P, MB, N], F32, 152)
        mrg = at("mrg", [P, KT, N], F32, 128)
        raw = at("raw", [P, RAW_SLOTS, CK, CB], F32, 160)
        wh = at("wh", [P, SPLIT_SLOTS, CK, CB], F32R, 176)
        wl = at("wl", [P, SPLIT_SLOTS, CK, CB], F32R, 184)
        sg = at("sg", [P, MB, N], F32, 192)

        ring = at("ring", [P, RING, EK, CB], F32, 96)
        xn = at("xn", [P, NT, D], F32, 160)
        g2bc = at("g2bc", [P, D], F32, 40)
        xb = at("xb", [P, 3, NT, D], BF16, 0)
        xt = at("xt", [P, 2, KT, P], F32, 48)
        xg = [at("xg0", [P, KT, P], F32, 48), at("xg1", [P, KT, P], F32, 184)]
        hh, sl = at("hh", [P, CB], F32, 56), at("sl", [P, CB], F32, 58)
        ht = at("ht", [P, EK, P], F32, 60)
        selb = at("selb", [P, NT, P], BF16, 62)
        self_ = at("self_", [P, NT, P], F32, 160)
        selt = at("selt", [P, NT, P], F32R, 162)
        yh, yl = at("yh", [P, 2, CB], F32R, 164), at("yl", [P, 2, CB], F32R, 168)
        fgbc = at("fgbc", [P, D], F32, 176)
        place = [192 * 1024]

        def rt(name, shape, dt=F32):
            t = nc.alloc_sbuf_tensor_at(name, shape, dt, offset=BASE + place[0])
            n = 4 if dt == F32 else 2
            for k in shape[1:]:
                n *= k
            place[0] += (n + 31) // 32 * 32
            assert place[0] <= 200 * 1024 - 64
            return t

        rw = rt("rw", [P, KT, EG + E])
        rb = rt("rb", [P, EG + E])
        lg = rt("lg", [P, NT, EG + E])
        gmax, gsum, gw, gtop = (rt(n, [P, NT, 1]) for n in ("gmax", "gsum", "gw", "gtop"))
        gsh, gexp, gcode, goh = (rt(n, [P, NT, EG]) for n in ("gsh", "gexp", "gcode", "goh"))
        emask = rt("emask", [P, NT, EG, EPG])
        esel, esh, eexp, ecode, oh1, es2, oh2, m8, p8 = (
            rt(n, [P, NT, EPG]) for n in ("esel", "esh", "eexp", "ecode", "oh1", "es2", "oh2", "m8", "p8"))
        emax, etop, den, rden = (rt(n, [P, NT, 1]) for n in ("emax", "etop", "den", "rden"))
        m32 = rt("m32", [P, NT, EG, EPG])
        m32b = rt("m32b", [P, NT, E], BF16)
        msum = rt("msum", [P, E])
        m128 = rt("m128", [P, E, P // E], BF16)
        active = rt("active", [P, 1])
        activeb = rt("activeb", [P, 1], BF16)
        prefix = rt("prefix", [P, 1])
        unit_oh = rt("unit_oh", [P, MAX_OVER])
        unit_ohb = rt("unit_ohb", [P, MAX_OVER], BF16)
        msumb = rt("msumb", [P, E], BF16)
        keys, ahead, unit_of, by_unit = (rt(n, [P, E]) for n in ("keys", "ahead", "unit_of", "by_unit"))
        key, rank, is_first, spot, spot2, own_flag, first_rank = (
            rt(n, [P, 1]) for n in ("key", "rank", "is_first", "spot", "spot2", "own_flag", "first_rank"))
        unit_ofb, full_ofb = rt("unit_ofb", [P, E], BF16), rt("full_ofb", [P, E], BF16)
        orderf, flags = rt("orderf", [P, PAIRS, 2]), rt("flags", [P, PAIRS])
        sharedf, notflag = rt("sharedf", [P, PAIRS]), rt("notflag", [P, PAIRS])
        unit_rb = rt("unit_rb", [P, MAX_OVER], BF16)
        over_nf = rt("over_nf", [P, 1])

        ps = ctx.enter_context(nc.psum_tensor("ps", [P, 8, CB], F32))

        x_in = [sem(f"x_in{m}") for m in range(NT)]
        g1_in = sem("g1_in")
        ws_in = sem("ws_in")
        small_in = sem("small_in")
        h_in = sem("h_in")
        raw_in = [sem(f"raw_in{s}") for s in range(RAW_SLOTS)]
        const_in, router_in, constb_ready = sem("const_in"), sem("router_in"), sem("constb_ready")
        warm_ready = sem("warm_ready")
        sq_done, rvar_ready, root_done, xn_ready = sem("sq_done"), sem("rvar_ready"), sem("root_done"), sem("xn_ready")
        tr_done, tr_hi, tr_lo = sem("tr_done"), sem("tr_hi"), sem("tr_lo")
        ws_masked, wst_tr, wst_ready = sem("ws_masked"), sem("wst_tr"), sem("wst_ready")
        hi_done, lo_done, pe_chunk = sem("hi_done"), sem("lo_done"), sem("pe_chunk")
        set_free = [sem("set_free0"), sem("set_free1")]
        v_gelu, v_ready = sem("v_gelu"), sem("v_ready")
        pad_zero = sem("pad_zero")
        ya_ready, yb_ready = sem("ya_ready"), sem("yb_ready")
        mixed_done, u_ready, u_used = sem("mixed_done"), sem("u_ready"), sem("u_used")
        sg_ready, mrg_sum = sem("sg_ready"), sem("mrg_sum")
        m_ready, h_ready = sem("m_ready"), [sem("h_ready0"), sem("h_ready1")]
        g2_in, fg_in = sem("g2_in"), sem("fg_in")
        xn2_ready, xb0_ready, xt_done, xt_ready, xb1_ready, xb2_ready, xr_done = (
            sem(n) for n in ("xn2_ready", "xb0_ready", "xt_done", "xt_ready", "xb1_ready", "xb2_ready", "xr_done"))
        logit_done, gsh_ready, gexp_ready, esh_ready, eexp_ready = (
            sem(n) for n in ("logit_done", "gsh_ready", "gexp_ready", "esh_ready", "eexp_ready"))
        mask_ready, rank_done, active_ready, prefix_done, unit_ready, table_done, table_ready = (
            sem(n) for n in ("mask_ready", "rank_done", "active_ready", "prefix_done", "unit_ready", "table_done",
                             "table_ready"))
        order_ready, order_done, pairs_ready = sem("order_ready"), sem("order_done"), sem("pairs_ready")
        ring_in = [sem(f"ring_in{s}") for s in range(RING)]
        sel_ready, gat_done, xg_done, seltr_done, selt_done = (
            sem(n) for n in ("sel_ready", "gat_done", "xg_done", "seltr_done", "selt_done"))
        used, silu_done, h_done, htr_done, ht_ready = (
            sem(n) for n in ("used", "silu_done", "h_done", "htr_done", "ht_ready"))
        yh_done, y_split, cb_done, add_done, moe_done = (
            sem(n) for n in ("yh_done", "y_split", "cb_done", "add_done", "moe_done"))
        out_ready = sem("out_ready")
        dve_step = sem("dve_step")
        stored = sem("stored")

        CREDITS = ((set_free[0], 1), (set_free[1], 1), (u_used, 1), (mrg_sum, 1), (sg_ready, 1), (h_ready[0], 1),
                   (h_ready[1], 1), (xg_done, 2), (y_split, 2), (add_done, NT), (cb_done, 5), (h_done, 1))

        block = ctx.enter_context(nc.Block())

        N_SMALL = 5

        @block.sync
        def _(sp):
            for m in range(NT):
                sp.dma_start(xnat[:, m], x_v[:, m]).then_inc(x_in[m], 16)
                if m == 0:
                    sp.dma_start(g1bc[:], norm1_g.partition_broadcast(P).rearrange("p o d -> p (o d)")).then_inc(g1_in, 16)

            def chunk(q, s):
                sp.dma_start(raw[:, s], mixer_w[bass.ds(q, 1)].rearrange("o p f -> (o p) f")).then_inc(raw_in[s], 16)

            for s in range(RAW_SLOTS):
                chunk(s, s)
            with sp.Fori(1, Q_OUT // RAW_SLOTS) as i:
                for s in range(RAW_SLOTS):
                    sp.wait_ge(lo_done, i * RAW_SLOTS + (s - RAW_SLOTS + 1))
                    chunk(i * RAW_SLOTS + s, s)
            def out_chunks(i):
                for s in range(RAW_SLOTS):
                    sp.wait_ge(lo_done, i * RAW_SLOTS + (s - RAW_SLOTS + 1))
                    chunk(i * RAW_SLOTS + s, s)

            def expert_chunk(q, s):
                sp.dma_start(ring[:, s].rearrange("p j n -> p (j n)"),
                             expert_w[bass.ds(q, 1)].rearrange("o p f -> (o p) f")).then_inc(ring_in[s], 16)

            lead, tail = Q_OUT // RAW_SLOTS + 2, Q_END // RAW_SLOTS - 2
            out_chunks(Q_OUT // RAW_SLOTS)
            sp.wait_ge(pe_chunk, Q_OUT)
            for m in range(NT):
                sp.dma_start(h[:, m], x_v[:, m]).then_inc(h_in, 16)
                if m == NT // 2 - 1:
                    out_chunks(Q_OUT // RAW_SLOTS + 1)
            sp.wait_ge(m_ready, KT)
            for i in range(lead, tail):
                out_chunks(i)
                for c in (2 * (i - lead), 2 * (i - lead) + 1):
                    expert_chunk((c % 2) * LX + c // 2, c)
            with sp.Fori(tail, Q_END // RAW_SLOTS) as i:
                out_chunks(i)
            sp.wait_ge(pe_chunk, Q_END)
            sp.dma_start(g2bc[:], norm2_g.partition_broadcast(P).rearrange("p o d -> p (o d)")).then_inc(g2_in, 16)

            def unit_chunks(u, first, last, expert):
                for c in range(first, last):
                    sp.wait_ge(used, u * USED + (c // 2 - RING // 2 + 1))
                    expert_chunk(expert(c % 2) * LX + c // 2, c % RING)

            def experts(u):
                return [sp.value_load(order[0:1, bass.ds(u * 2 + ab, 1)], min_val=0, max_val=E - 1) for ab in range(2)]

            sp.wait_ge(pairs_ready, 1)
            with sp.Fori(0, PAIRS - 1) as u:
                e = experts(u)
                unit_chunks(u, RING, 2 * LX, lambda ab: e[ab])
                e = experts(u + 1)
                unit_chunks(u + 1, 0, RING, lambda ab: e[ab])
            e = [sp.value_load(order[0:1, E - 2 + ab:E - 1 + ab], min_val=0, max_val=E - 1) for ab in range(2)]
            for c in range(RING, 2 * LX):
                sp.wait_ge(used, (PAIRS - 1) * USED + c // 2 - RING // 2 + 1)
                expert_chunk(e[c % 2] * LX + c // 2, c % RING)
            sp.wait_ge(sel_ready, 1)
            sp.dma_start(fgbc[:], final_g.partition_broadcast(P).rearrange("p o d -> p (o d)")).then_inc(fg_in, 16)
            sp.wait_ge(table_ready, 1)
            n_over = sp.value_load(over_n[0:1, 0:1], min_val=0, max_val=MAX_OVER - 1)
            with sp.Fori(0, MAX_OVER - 1) as i:
                with sp.If(i < n_over):
                    e = sp.value_load(over_e[0:1, bass.ds(i, 1)], min_val=0, max_val=E - 1)
                    for l in range(LX):
                        sp.wait_ge(used, (i + PAIRS) * USED + (l - RING // 2 + 1))
                        expert_chunk(e * LX + l, 2 * l % RING)
            for m in range(NT):
                sp.wait_ge(out_ready, m + 1)
                sp.dma_start(out_v[:, m], h[:, m]).then_inc(stored, 16)
            sp.wait_ge(stored, 16 * NT)

        @block.gpsimd
        def _(pool):
            pool.wait_ge(ws_in, 16)
            nc.gpsimd.affine_select(out=wsraw[:], in_=wsraw[:], compare_op=ALU.is_ge, fill=0.0, base=0,
                                    pattern=[[0, G], [-1, P]], channel_multiplier=1).then_inc(ws_masked, 1)

            with pool.Fori(0, Q_END // RAW_SLOTS) as i:
                for c in range(RAW_SLOTS):
                    pool.wait_ge(hi_done, i * RAW_SLOTS + c + 1)
                    s = c % SPLIT_SLOTS
                    nc.gpsimd.tensor_tensor(wl[:, s], raw[:, c], wh[:, s].bitcast(F32), ALU.subtract).then_inc(lo_done, 1)

            for m in range(NT):
                pool.wait_ge(xb1_ready, m + 1)
                nc.gpsimd.tensor_tensor(xb[:, 2, m], xn[:, m], xb[:, 1, m], ALU.subtract).then_inc(xb2_ready, 1)

        @block.scalar
        def _(act):
            act.dma_start(const[:], consts).then_inc(const_in, 16)
            act.dma_start(wsraw[:], sgu_w[0].rearrange("g t s -> t g s")).then_inc(ws_in, 16)

            def preload(func, k):
                act.wait_ge(warm_ready, 1)
                nc.scalar.activation(warm[:, k:k + 1], warm[:, 0:1], func)

            def square(m, cols, acc, n):
                if n > 1:
                    act.wait_ge(sq_done, n - 1)
                nc.scalar.activation(ps[:, 0:4].rearrange("p a b -> p (a b)")[:, 0:cols.shape[1]], cols, ACT.Square,
                                     accum_out=acc[:, m:m + 1]).then_inc(sq_done, 1)

            def root(m, n):
                act.wait_ge(rvar_ready, n)
                nc.scalar.activation(rstd[:, m], rvar[:, m], ACT.Sqrt).then_inc(root_done, 1)

            def turned(m):
                for kc in range(KT // 4):
                    t = m * (KT // 4) + kc
                    act.wait_ge(tr_done, t + 1)
                    nc.scalar.activation(xh[:, 4 * kc:4 * kc + 4, m * P:(m + 1) * P],
                                         ps[:, 4 + t % 4].rearrange("p (k n) -> p k n", k=4), ACT.Copy).then_inc(tr_hi, 1)

            def hi(q, c):
                if isinstance(q, int):
                    use = (q + c) // RAW_SLOTS + 1
                else:
                    use = q // RAW_SLOTS + c // RAW_SLOTS + 1
                act.wait_ge(raw_in[c % RAW_SLOTS], use * 16)
                if not isinstance(q, int) or q + c >= SPLIT_SLOTS:
                    act.wait_ge(pe_chunk, q + c - SPLIT_SLOTS + 1)
                nc.scalar.activation(wh[:, c % SPLIT_SLOTS], raw[:, c % RAW_SLOTS], ACT.Copy).then_inc(hi_done, 1)

            def hi_at(i, q0, per, c):
                act.wait_ge(raw_in[c % RAW_SLOTS], i * (16 * per // RAW_SLOTS) + 16 * ((q0 + c) // RAW_SLOTS + 1))
                act.wait_ge(pe_chunk, i * per + (q0 + c - SPLIT_SLOTS + 1))
                nc.scalar.activation(wh[:, c % SPLIT_SLOTS], raw[:, c % RAW_SLOTS], ACT.Copy).then_inc(hi_done, 1)

            preload(ACT.Sqrt, 1)
            for m in range(NT):
                act.wait_ge(x_in[m], 16)
                square(m, xnat[:, m], sumsq, m + 1)
                root(slice(m, m + 1), m + 1)
                if m == NT - 1:
                    act.dma_start(bgate[:], b_gate).then_inc(small_in, 16)
                    act.dma_start(convw[:], conv_w).then_inc(small_in, 16)
                    act.dma_start(lng[:], ln_v_g.partition_broadcast(P).rearrange("p o d -> p (o d)")).then_inc(small_in, 16)
                    act.dma_start(lnb[:], ln_v_b.partition_broadcast(P).rearrange("p o d -> p (o d)")).then_inc(small_in, 16)
                    act.dma_start(sgub[:], sgu_b.partition_broadcast(P).rearrange("p o g t -> p (o g) t")).then_inc(small_in, 16)
                if m >= 1:
                    turned(m - 1)
            hi(0, 0)
            turned(NT - 1)
            hi(0, 1)
            for i in range(WB):
                for c in range(KC):
                    hi(Q_V + i * KC, 2 + c)
                for m in range(MB):
                    act.wait_ge(pe_chunk, Q_V + (i + 1) * KC)
                    nc.scalar.activation(v[:, m, i * CB:(i + 1) * CB], ps[:, 4 * i + m], ACT.Gelu_apprx_tanh
                                         ).then_inc(v_gelu, 1)
            root(slice(0, NT), NT + 1)
            with act.Fori(0, WB) as i:
                for c in range(3 * KC):
                    hi_at(i, Q_CONV, 3 * KC, 2 + c)
            with act.Fori(0, WB) as i:
                for c in range(KC):
                    hi_at(i, Q_U, KC, 2 + c)
                act.wait_ge(pe_chunk, i * KC + Q_U + KC)
                act.wait_ge(u_used, i + 1)
                for m in range(MB):
                    nc.scalar.activation(sg[:, m], ps[:, m], ACT.Gelu_apprx_tanh).then_inc(u_ready, 1)
            with act.Fori(0, DB) as i:
                for r in range(2):
                    q = r * (KC + WC)
                    for c in range(KC):
                        hi_at(i, Q_MERGE, 2 * (KC + WC), q + 2 + c)
                    act.wait_ge(pe_chunk, i * 2 * (KC + WC) + (Q_MERGE + q + KC))
                    if r == 0:
                        act.wait_ge(u_used, WB + 1)
                        act.wait_ge(mrg_sum, i + 1)
                    else:
                        act.wait_ge(set_free[1], 2 * i + (2 * WB + 2))
                    for m in range(MB):
                        nc.scalar.activation(sg[:, m], ps[:, m], ACT.Sigmoid,
                                             bias=bgate[:, bass.ds(i * MB + r * KT + m, 1)]).then_inc(sg_ready, 1)
                    for c in range(WC):
                        hi_at(i, Q_MERGE, 2 * (KC + WC), q + KC + 2 + c)
            with act.Fori(0, DB - 1) as i:
                for c in range(KC):
                    hi_at(i, Q_OUT, KC, 2 + c)
            for c in range(2, KC):
                hi(Q_OUT + (DB - 1) * KC, c)

            preload(ACT.Sqrt, 2)
            for m in range(NT):
                act.wait_ge(h_ready[1], NT * (DB // 2 - 1) + 1)
                act.wait_ge(h_ready[0], NT * (DB // 2) + 1)
                square(m, h[:, m, 0:D - CB], sumsq, NT + m + 1)
            for m in range(NT):
                act.wait_ge(h_ready[1], NT * (DB // 2 - 1) + m + 2)
                square(m, h[:, m, D - CB:D], sumsq2, 2 * NT + m + 1)
            for m in range(NT):
                root(slice(m, m + 1), NT + 1 + m + 1)
            act.dma_start(rw[:], router_w).then_inc(router_in, 16)
            act.dma_start(rb[:], router_b.partition_broadcast(P).rearrange("p o d -> p (o d)")).then_inc(router_in, 16)
            for m in range(NT):
                for kc in range(KT // 4):
                    t = m * (KT // 4) + kc
                    act.wait_ge(xt_done, t + 1)
                    if m >= 2:
                        act.wait_ge(logit_done, m - 1)
                    nc.scalar.activation(xt[:, m % 2, 4 * kc:4 * kc + 4], ps[:, 4 + t % 4].rearrange("p (k n) -> p k n", k=4),
                                         ACT.Copy).then_inc(xt_ready, 1)
                nc.scalar.activation(xb[:, 0, m], xn[:, m], ACT.Copy).then_inc(xb0_ready, 1)
            preload(ACT.Exp, 3)
            act.wait_ge(gsh_ready, 1)
            nc.scalar.activation(gexp[:], gsh[:], ACT.Exp).then_inc(gexp_ready, 1)
            act.wait_ge(esh_ready, 1)
            nc.scalar.activation(eexp[:], esh[:], ACT.Exp).then_inc(eexp_ready, 1)

            def gathered(u, p):
                for kc in range(KT // 4):
                    act.wait_ge(gat_done, u * (KT // 4) + (kc + 1))
                    nc.scalar.activation(xg[p][:, 4 * kc:4 * kc + 4], ps[:, 6 + kc % 2].rearrange("p (k n) -> p k n", k=4),
                                         ACT.Copy).then_inc(xg_done, 1)

            def silu(u):
                act.wait_ge(used, u * USED + (2 * KX - 1))
                act.wait_ge(h_done, u + 1)
                nc.scalar.activation(sl[:], ps[:, 0], ACT.Silu).then_inc(silu_done, 1)

            def high_y(u):
                for c in range(DX):
                    act.wait_ge(used, u * USED + (2 * KX + c + 1))
                    act.wait_ge(cb_done, u * 4 * NT + (NT * c - NT + 5 if c else 1))
                    nc.scalar.activation(yh[:, c % 2], ps[:, 2 + c % 2], ACT.Copy).then_inc(yh_done, 1)

            def first_products(u):
                act.wait_ge(used, u * USED + 1)

            gathered(0, 0)
            with act.Fori(0, PAIRS // 2 - 1) as w:
                for p in range(2):
                    u = w * 2 + p
                    first_products(u)
                    gathered(u + 1, 1 - p)
                    silu(u)
                    high_y(u)
            first_products(PAIRS - 2)
            gathered(PAIRS - 1, 1)
            silu(PAIRS - 2)
            high_y(PAIRS - 2)
            silu(PAIRS - 1)
            high_y(PAIRS - 1)
            act.wait_ge(table_ready, 1)
            n_over = act.value_load(over_n[0:1, 0:1], min_val=0, max_val=MAX_OVER - 1)
            with act.Fori(0, MAX_OVER - 1) as i:
                with act.If(i < n_over):
                    gathered(i + PAIRS, 0)
                    silu(i + PAIRS)
                    high_y(i + PAIRS)
            act.wait_ge(moe_done, 1)
            for m in range(NT):
                square(m, h[:, m], sumsq, 3 * NT + m + 1)
                root(slice(m, m + 1), 2 * NT + 1 + m + 1)

        @block.tensor
        def _(pe):
            pe.wait_ge(const_in, 16)
            for t in range(NT * KT // 4):
                m, kc = t // (KT // 4), t % (KT // 4)
                pe.wait_ge(xn_ready, m + 1)
                if t >= 4:
                    pe.wait_ge(tr_lo, t - 3)
                for j in range(4):
                    k = 4 * kc + j
                    last = nc.tensor.transpose(ps[:, 4 + t % 4, j * P:(j + 1) * P], xnat[:, m, k * P:(k + 1) * P], ident)
                last.then_inc(tr_done, 1)
            pe.wait_ge(ws_masked, 1)
            pe.wait_ge(sq_done, NT)
            for g in range(G):
                last = nc.tensor.transpose(ps[:, g // 4, (g % 4) * P:(g % 4 + 1) * P], wsraw[:, g], ident)
            last.then_inc(wst_tr, 1)
            pe.wait_ge(wst_ready, 1)
            pe.wait_ge(tr_lo, NT * KT // 4)

            def channel_block(ah, al, kts, base, q):
                for c in range(kts // CK):
                    pe.wait_ge(lo_done, q + c + 1)
                    for j in range(CK):
                        k = c * CK + j
                        for m in range(MB):
                            o = ps[:, base + m]
                            whi = wh[:, c % SPLIT_SLOTS, j, m * P:(m + 1) * P]
                            wlo = wl[:, c % SPLIT_SLOTS, j, m * P:(m + 1) * P]
                            nc.tensor.matmul(o, whi, ah[:, k], start=(k == 0), stop=False)
                            nc.tensor.matmul(o, whi, al[:, k], start=False, stop=False)
                            last = nc.tensor.matmul(o, wlo, ah[:, k], start=False, stop=(k == kts - 1))
                    last.then_inc(pe_chunk, 1)

            def token_block(ah, al, base, q, ready=None):
                for c in range(KC):
                    pe.wait_ge(lo_done, q + c + 1)
                    for j in range(CK):
                        k = c * CK + j
                        if ready is not None:
                            pe.wait_ge(ready, k + 1)
                        for m in range(NT):
                            o = ps[:, base + m]
                            xhi = ah[:, k, m * P:(m + 1) * P]
                            xlo = al[:, k, m * P:(m + 1) * P]
                            nc.tensor.matmul(o, xhi, wh[:, c % SPLIT_SLOTS, j], start=(k == 0), stop=False)
                            nc.tensor.matmul(o, xhi, wl[:, c % SPLIT_SLOTS, j], start=False, stop=False)
                            last = nc.tensor.matmul(o, xlo, wh[:, c % SPLIT_SLOTS, j], start=False, stop=(k == KT - 1))
                    last.then_inc(pe_chunk, 1)

            for i in range(WB):
                token_block(xh, xl, 4 * i, Q_V + i * KC)
            with pe.Fori(0, WB) as i:
                q = i * 3 * KC + Q_CONV
                pe.wait_ge(v_gelu, MB * WB)
                pe.wait_ge(set_free[0], 2 * i + 1)
                channel_block(xh, xl, KT, 0, q)
                pe.wait_ge(set_free[1], i + 1)
                channel_block(xh, xl, KT, 4, q + KC)
                pe.wait_ge(set_free[0], 2 * i + 2)
                channel_block(xh, xl, KT, 0, q + 2 * KC)
            for i in range(WB):
                pe.wait_ge(v_ready, NT)
                pe.wait_ge(set_free[1], WB + i + 1)
                for m in range(MB):
                    g = i * MB + m
                    for n in range(NT):
                        last = nc.tensor.matmul(ps[:, 4 + m, n * P:(n + 1) * P], v[:, n, g * P:(g + 1) * P],
                                                wst[:, g], start=True, stop=True)
                last.then_inc(mixed_done, 1)
                if i == 0:
                    pe.wait_ge(set_free[0], 2 * WB + 1)
                else:
                    pe.wait_ge(u_ready, MB * i)
                channel_block(xh, xl, KT, 0, Q_U + i * KC)
            with pe.Fori(0, DB) as i:
                for r in range(2):
                    q = i * 2 * (KC + WC) + (Q_MERGE + r * (KC + WC))
                    pe.wait_ge(u_ready, MB * WB)
                    pe.wait_ge(sg_ready, i * 2 * MB + (MB * r + 1))
                    channel_block(xh, xl, KT, 0, q)
                    pe.wait_ge(ya_ready if r == 0 else yb_ready, WB)
                    pe.wait_ge(set_free[1], i * 2 + (2 * WB + r + 1))
                    channel_block(yah if r == 0 else ybh, yal if r == 0 else ybl, WT, 4, q + KC)
            with pe.Fori(0, DB // 2) as i:
                for s in range(2):
                    if s == 0:
                        pe.wait_ge(sg_ready, 2 * MB * DB + 1)
                    else:
                        pe.wait_ge(set_free[1], 2 * WB + 2 * DB + 1)
                    pe.wait_ge(h_ready[s], i * NT + 1)
                    token_block(mh, ml, 4 * s, i * 2 * KC + (Q_OUT + s * KC), ready=m_ready)

            for m in range(NT):
                for kc in range(KT // 4):
                    t = m * (KT // 4) + kc
                    pe.wait_ge(xn2_ready, m + 1)
                    if t >= 4:
                        pe.wait_ge(xt_ready, t - 3)
                    else:
                        pe.wait_ge(h_ready[1], NT * (DB // 2) + 1)
                    for j in range(4):
                        k = 4 * kc + j
                        last = nc.tensor.transpose(ps[:, 4 + t % 4, j * P:(j + 1) * P], xn[:, m, k * P:(k + 1) * P], ident)
                    last.then_inc(xt_done, 1)
                pe.wait_ge(router_in, 32)
                pe.wait_ge(sq_done, 3 * NT)
                for k in range(KT):
                    if k % 4 == 0:
                        pe.wait_ge(xt_ready, m * (KT // 4) + k // 4 + 1)
                    last = nc.tensor.matmul(ps[:, m, 0:EG + E], xt[:, m % 2, k], rw[:, k], start=(k == 0), stop=(k == KT - 1))
                last.then_inc(logit_done, 1)

            pe.wait_ge(constb_ready, 1)
            pe.wait_ge(mask_ready, 1)
            pe.wait_ge(xt_ready, NT * KT // 4)
            for n in range(NT):
                for b in range(n + 1):
                    nc.tensor.matmul(ps[:, 4, n * E:(n + 1) * E], before if b == n else ones, m32b[:, b],
                                     start=(b == 0), stop=(b == n))
            nc.tensor.matmul(ps[:, 5, 0:1], m128[:].rearrange("p e t -> p (e t)"), ones[:, 0:1], start=True, stop=True)
            nc.tensor.matmul(ps[:, 6, 0:E], ones, msumb[:], start=True, stop=True).then_inc(rank_done, 1)
            pe.wait_ge(order_ready, 1)
            nc.tensor.matmul(ps[:, 7, 0:E], cand_e, unit_ofb[:], start=True, stop=True)
            nc.tensor.matmul(ps[:, 7, E:2 * E], ones, full_ofb[:], start=True, stop=True).then_inc(order_done, 1)

            def further_units():
                pe.wait_ge(active_ready, 1)
                nc.tensor.matmul(ps[:, 5, 2:3], before, activeb[:], start=True, stop=True).then_inc(prefix_done, 1)
                pe.wait_ge(unit_ready, 1)
                for k, (t, what) in enumerate(((cand_e, unit_ohb), (ones, unit_rb), (ones, unit_ohb))):
                    last = nc.tensor.matmul(ps[:, 4, k * MAX_OVER:(k + 1) * MAX_OVER], t, what[:], start=True, stop=True)
                last.then_inc(table_done, 1)
                pe.wait_ge(table_ready, 1)

            SHARED, SECOND, FIRST = slice(0, TILE), slice(TILE, 2 * TILE), slice(CAP, 2 * CAP)

            def pair_product(bank, lhs, l, j, s, first, end):
                a = 2 * l % RING
                for tile, w in ((FIRST, ring[:, a, j]), (SHARED, ring[:, bass.ds(s + a, 1), j].rearrange("p o n -> p (o n)")),
                                (SECOND, ring[:, a + 1, j])):
                    last = nc.tensor.matmul(ps[tile, bank], lhs[:, tile], w, start=first, stop=end, skip_group_check=True)
                return last

            def gather(u, first, last_kc):
                for kc in range(first, last_kc):
                    pe.wait_ge(sel_ready, u + 1)
                    pe.wait_ge(xg_done, u * (KT // 4) + (kc + 1))
                    for j in range(4):
                        k = 4 * kc + j
                        for n in range(NT):
                            for b in range(3):
                                last = nc.tensor.matmul(ps[:, 6 + kc % 2, j * P:(j + 1) * P], xb[:, b, n, k * P:(k + 1) * P],
                                                        selb[:, n], start=(n == 0 and b == 0), stop=(n == NT - 1 and b == 2))
                    last.then_inc(gat_done, 1)

            def added(u):
                pe.wait_ge(add_done, u * (DX * NT) + NT)

            def turn_selection(u):
                added(u)
                pe.wait_ge(xg_done, (u + 1) * (KT // 4) + 2)
                for n in range(NT):
                    nc.tensor.transpose(ps[:, 6, n * P:(n + 1) * P], self_[:, n], ident)
                for n in range(NT):
                    last = nc.tensor.matmul(ps[:, 7, 0:3], self_[:, n], wc[:, n], start=(n == 0), stop=(n == NT - 1))
                last.then_inc(seltr_done, 1)

            def landed(u, c):
                pe.wait_ge(ring_in[c % RING], u * (2 * LX // RING * 16) + (c // RING + 1) * 16)

            def gate_up(u, p, l, s=None):
                landed(u, 2 * l)
                if s is not None:
                    landed(u, 2 * l + 1)
                kc = l // 2
                for j in range(EK):
                    first, end = kc == 0 and j == 0, kc == KX - 1 and j == EK - 1
                    if s is not None:
                        last = pair_product(l % 2, xg[p][:, EK * kc + j], l, j, s, first, end)
                    else:
                        last = nc.tensor.matmul(ps[:, l % 2], xg[p][:, EK * kc + j], ring[:, 2 * l % RING, j],
                                                start=first, stop=end)
                last.then_inc(used, 1)

            def turn_hidden(u):
                pe.wait_ge(h_done, u + 2)
                for j in range(EK):
                    last = nc.tensor.transpose(ps[:, 0, j * P:(j + 1) * P], hh[:, j * P:(j + 1) * P], ident)
                last.then_inc(htr_done, 1)
                pe.wait_ge(ht_ready, u + 1)

            def down(u, c, s=None):
                l = 2 * KX + c
                landed(u, 2 * l)
                if s is not None:
                    landed(u, 2 * l + 1)
                pe.wait_ge(y_split, u * DX + (c + 1))
                for j in range(EK):
                    if s is not None:
                        last = pair_product(2 + c % 2, ht[:, j], l, j, s, j == 0, j == EK - 1)
                    else:
                        last = nc.tensor.matmul(ps[:, 2 + c % 2], ht[:, j], ring[:, 2 * l % RING, j],
                                                start=(j == 0), stop=(j == EK - 1))
                last.then_inc(used, 1)

            def combine(u, c):
                pe.wait_ge(y_split, u * DX + (c + 3))
                for n in range(NT):
                    pe.wait_ge(add_done, u * (DX * NT) + (c * NT + n + 1))
                    nc.tensor.matmul(ps[:, 4 + n], selt[:, n], yh[:, c % 2], start=True, stop=False)
                    nc.tensor.matmul(ps[:, 4 + n], selt[:, n], yl[:, c % 2], start=False, stop=True).then_inc(cb_done, 1)

            def back(u, gathered, s=None):
                pe.wait_ge(selt_done, u + 1)
                down(u, 0, s)
                pe.wait_ge(xg_done, gathered * (KT // 4) + 2)
                for c in range(1, DX):
                    down(u, c, s)
                    combine(u, c - 1)
                combine(u, DX - 1)

            def pair_unit(u, p, more):
                s = pe.value_load(shared_b[0:1, bass.ds(u, 1)], min_val=0, max_val=1)
                gate_up(u, p, 0, s)
                turn_selection(u)
                gate_up(u, p, 1, s)
                for l in range(2, 2 * KX):
                    gate_up(u, p, l, s)
                    if more and l < 2 + KT // 4:
                        pe.wait_ge(selt_done, u + 1)
                        gather(u + 1, l - 2, l - 1)
                turn_hidden(u)
                back(u, u + 2 if more else u + 1, s)

            pe.wait_ge(xb0_ready, NT)
            pe.wait_ge(xb1_ready, NT)
            pe.wait_ge(xb2_ready, NT)
            gather(0, 0, KT // 4)
            further_units()
            with pe.Fori(0, PAIRS // 2 - 1) as w:
                for p in range(2):
                    pair_unit(w * 2 + p, p, more=True)
            pair_unit(PAIRS - 2, 0, more=True)
            pair_unit(PAIRS - 1, 1, more=False)
            n_over = pe.value_load(over_n[0:1, 0:1], min_val=0, max_val=MAX_OVER - 1)
            with pe.Fori(0, MAX_OVER - 1) as i:
                with pe.If(i < n_over):
                    u = i + PAIRS
                    added(u)
                    gather(u, 0, KT // 4)
                    turn_selection(u)
                    for l in range(2 * KX):
                        gate_up(u, 0, l)
                    turn_hidden(u)
                    back(u, u + 1)

        @block.vector
        def _(dve):
            for s, credit in CREDITS:
                dve.sem_inc(s, credit)
            nc.vector.memset(warm[:], 1.0).then_inc(warm_ready, 1)
            step = [0]

            def link(ins):
                step[0] += 1
                ins.then_inc(dve_step, 1)
                dve.wait_ge(dve_step, step[0])

            def finish_root(m, n, link=link):
                nc.vector.reciprocal(rvar[:, m], var[:, m]).then_inc(rvar_ready, 1)
                dve.wait_ge(root_done, n)
                link(nc.vector.tensor_tensor(rvar[:, m], rstd[:, m], rstd[:, m], ALU.mult))
                link(nc.vector.tensor_tensor(rvar[:, m], rvar[:, m], var[:, m], ALU.mult))
                link(nc.vector.tensor_scalar(rvar[:, m], rvar[:, m], -0.5, 1.5, ALU.mult, ALU.add))
                link(nc.vector.tensor_tensor(rstd[:, m], rstd[:, m], rvar[:, m], ALU.mult))

            def norm(m, squares_done, n, link=link):
                m = slice(m, m + 1)
                dve.wait_ge(sq_done, squares_done)
                link(nc.vector.tensor_scalar(var[:, m], sumsq[:, m], 1.0 / D, EPS, ALU.mult, ALU.add))
                finish_root(m, n, link)

            def turned_low(m):
                for kc in range(KT // 4):
                    t = m * (KT // 4) + kc
                    dve.wait_ge(tr_hi, t + 1)
                    dst = slice(4 * kc, 4 * kc + 4), slice(m * P, (m + 1) * P)
                    nc.vector.tensor_tensor(xl[:, dst[0], dst[1]], ps[:, 4 + t % 4].rearrange("p (k n) -> p k n", k=4),
                                            xh[:, dst[0], dst[1]].bitcast(F32), ALU.subtract).then_inc(tr_lo, 1)

            dve.wait_ge(const_in, 16)
            nc.vector.tensor_copy(constb[:].rearrange("p a b -> p (a b)"), wide).then_inc(constb_ready, 1)
            for m in range(NT):
                norm(m, m + 1, m + 1)
                dve.wait_ge(g1_in, 16)
                nc.vector.scalar_tensor_tensor(out=xnat[:, m], in0=xnat[:, m], scalar=rstd[:, m:m + 1], in1=g1bc[:],
                                               op0=ALU.mult, op1=ALU.mult).then_inc(xn_ready, 1)
                if m >= 1:
                    turned_low(m - 1)
            turned_low(NT - 1)
            dve.wait_ge(wst_tr, 1)
            nc.vector.tensor_copy(wst[:].rearrange("p g t -> p (g t)"), ps[:, 0:2].rearrange("p a b -> p (a b)")
                                  ).then_inc(wst_ready, 1)

            for m in range(NT):
                dve.wait_ge(v_gelu, NT * (WB - 1) + m + 1)
                for b in range(WB):
                    last = nc.vector.bn_stats(bnst[:, m, b], v[:, m, b * CB:(b + 1) * CB])
                link(last)
                link(nc.vector.bn_aggr(bnag[:, m], bnst[:, m].rearrange("p a b -> p (a b)")))
            link(nc.vector.tensor_scalar(var[:], bnag[:, :, 1:2].rearrange("p m o -> p (m o)"), EPS, None, ALU.add))
            finish_root(slice(0, NT), NT + 1)
            dve.wait_ge(small_in, 16 * N_SMALL)
            for m in range(NT):
                link(nc.vector.tensor_scalar(v[:, m], v[:, m], bnag[:, m, 0:1], rstd[:, m:m + 1], ALU.subtract, ALU.mult))
                link(nc.vector.tensor_tensor(v[:, m], v[:, m], lng[:], ALU.mult))
                nc.vector.tensor_tensor(v[:, m], v[:, m], lnb[:], ALU.add).then_inc(v_ready, 1)
            nc.vector.memset(xc[:, :, 0:2], 0.0).then_inc(pad_zero, 1)

            def chain_in(i, per, base):
                local = [0]

                def chain(ins):
                    local[0] += 1
                    ins.then_inc(dve_step, 1)
                    dve.wait_ge(dve_step, i * per + (base + local[0]))
                return chain

            CONV_STEPS = 4
            with dve.Fori(0, WB) as i:
                chain = chain_in(i, CONV_STEPS, step[0])
                q = i * 3 * KC + Q_CONV
                dve.wait_ge(pe_chunk, q + KC)
                for m in range(MB):
                    last = nc.vector.tensor_copy(cbuf[:, m], ps[:, m])
                last.then_inc(set_free[0], 1)
                dve.wait_ge(set_free[0], 2 * i + 2)
                dve.wait_ge(pe_chunk, q + 2 * KC)
                dve.wait_ge(pad_zero, 1)
                for m in range(MB):
                    last = nc.vector.tensor_tensor(xc[:, m, 2:N + 2], ps[:, 4 + m], cbuf[:, m], ALU.mult)
                last.then_inc(set_free[1], 1)
                dve.wait_ge(set_free[1], i + 2)
                for k in (2, 1, 0):
                    for m in range(MB):
                        w = convw[:, k, bass.ds(i * MB + m, 1)]
                        if k == 2:
                            last = nc.vector.tensor_scalar(cbuf[:, m], xc[:, m, 2:N + 2], w, None, ALU.mult)
                        else:
                            last = nc.vector.scalar_tensor_tensor(out=cbuf[:, m], in0=xc[:, m, k:k + N], scalar=w,
                                                                  in1=cbuf[:, m], op0=ALU.mult, op1=ALU.add)
                    chain(last)
                dve.wait_ge(pe_chunk, q + 3 * KC)
                for m in range(MB):
                    last = nc.vector.tensor_tensor(cbuf[:, m], ps[:, m], cbuf[:, m], ALU.mult)
                last.then_inc(set_free[0], 1)
                dve.wait_ge(set_free[0], 2 * i + 3)
                mine = bass.ds(i * MB, MB)
                chain(nc.vector.tensor_copy(yah[:, mine], cbuf[:]))
                nc.vector.tensor_tensor(yal[:, mine], cbuf[:], yah[:, mine].bitcast(F32), ALU.subtract
                                        ).then_inc(ya_ready, 1)
                dve.wait_ge(ya_ready, i + 1)
            step[0] += WB * CONV_STEPS

            SGU_STEPS = 1
            with dve.Fori(0, WB) as i:
                chain = chain_in(i, SGU_STEPS, step[0])
                dve.wait_ge(mixed_done, i + 1)
                for m in range(MB):
                    bias = sgub[:, bass.ds(i * MB + m, 1)].to_broadcast([P, NT, P])
                    last = nc.vector.tensor_tensor(mx[:, m].rearrange("p (n t) -> p n t", n=NT),
                                                   ps[:, 4 + m].rearrange("p (n t) -> p n t", n=NT), bias, ALU.add)
                last.then_inc(set_free[1], 1)
                dve.wait_ge(set_free[1], i + (WB + 2))
                dve.wait_ge(u_ready, MB * i + MB)
                nc.vector.tensor_tensor(mx[:], mx[:], sg[:], ALU.mult).then_inc(u_used, 1)
                dve.wait_ge(u_used, i + 2)
                mine = bass.ds(i * MB, MB)
                chain(nc.vector.tensor_copy(ybh[:, mine], mx[:]))
                nc.vector.tensor_tensor(ybl[:, mine], mx[:], ybh[:, mine].bitcast(F32), ALU.subtract
                                        ).then_inc(yb_ready, 1)
                dve.wait_ge(yb_ready, i + 1)
            step[0] += WB * SGU_STEPS

            def merge(i, r):
                mine = bass.ds(i * MB, MB)
                dve.wait_ge(pe_chunk, i * 2 * (KC + WC) + (Q_MERGE + (r + 1) * (KC + WC)))
                dve.wait_ge(sg_ready, i * 2 * MB + (MB * (r + 1) + 1))
                if r == 0:
                    nc.vector.tensor_tensor(mrg[:, mine], ps[:, 4:8], sg[:], ALU.mult).then_inc(set_free[1], 1)
                else:
                    nc.vector.tensor_tensor(sg[:], ps[:, 4:8], sg[:], ALU.mult).then_inc(set_free[1], 1)
                    dve.wait_ge(set_free[1], i * 2 + (2 * WB + 3))
                    nc.vector.tensor_tensor(mrg[:, mine], mrg[:, mine], sg[:], ALU.add).then_inc(mrg_sum, 1)
                    dve.wait_ge(mrg_sum, i + 2)

            def split_merged(first, last):
                for k in range(first, last):
                    link(nc.vector.tensor_copy(mh[:, k], mrg[:, k]))
                    nc.vector.tensor_tensor(ml[:, k], mrg[:, k], mh[:, k].bitcast(F32), ALU.subtract).then_inc(m_ready, 1)

            with dve.Fori(0, DB - 1) as i:
                for r in range(2):
                    merge(i, r)
            merge(DB - 1, 0)
            dve.wait_ge(pe_chunk, Q_OUT - WC)
            split_merged(0, KT - MB)
            merge(DB - 1, 1)
            split_merged(KT - MB, KT)
            dve.wait_ge(h_in, 16 * NT)
            with dve.Fori(0, DB // 2) as i:
                for s in range(2):
                    dve.wait_ge(pe_chunk, i * 2 * KC + (Q_OUT + (s + 1) * KC))
                    for m in range(NT):
                        hs = h[:, m, bass.ds(i * 2 * CB + s * CB, CB)]
                        nc.vector.tensor_tensor(hs, hs, ps[:, 4 * s + m], ALU.add).then_inc(h_ready[s], 1)

            dve.wait_ge(g2_in, 16)
            for m in range(NT):
                dve.wait_ge(sq_done, 2 * NT + m + 1)
                link(nc.vector.tensor_tensor(sumsq[:, m:m + 1], sumsq[:, m:m + 1], sumsq2[:, m:m + 1], ALU.add))
                norm(m, 2 * NT + m + 1, NT + 1 + m + 1)
                nc.vector.scalar_tensor_tensor(out=xn[:, m], in0=h[:, m], scalar=rstd[:, m:m + 1], in1=g2bc[:],
                                               op0=ALU.mult, op1=ALU.mult).then_inc(xn2_ready, 1)
            for m in range(NT):
                dve.wait_ge(xb0_ready, m + 1)
                dve.wait_ge(xt_done, (m + 1) * (KT // 4))
                nc.vector.tensor_tensor(xn[:, m], xn[:, m], xb[:, 0, m], ALU.subtract).then_inc(xr_done, 1)
                dve.wait_ge(xr_done, m + 1)
                nc.vector.tensor_copy(xb[:, 1, m], xn[:, m]).then_inc(xb1_ready, 1)
            dve.wait_ge(router_in, 32)
            dve.wait_ge(logit_done, NT)
            for m in range(NT):
                last = nc.vector.tensor_tensor(lg[:, m], ps[:, m, 0:EG + E], rb[:], ALU.add)
            link(last)

            def wide_n(ap, k):
                return ap.to_broadcast([P, NT, k])

            def top(dst, code, best):
                link(nc.vector.tensor_reduce(best[:], code[:], AX, ALU.max))
                link(nc.vector.tensor_tensor(dst[:], code[:], wide_n(best[:], code.shape[2]), ALU.is_equal))

            gl = lg[:, :, 0:EG]
            link(nc.vector.tensor_reduce(gmax[:], gl, AX, ALU.max))
            nc.vector.tensor_tensor(gsh[:], gl, wide_n(gmax[:], EG), ALU.subtract).then_inc(gsh_ready, 1)
            dve.wait_ge(gsh_ready, 1)
            link(nc.vector.scalar_tensor_tensor(out=gcode[:], in0=gsh[:], scalar=0.0, in1=desc_g.unsqueeze(1).to_broadcast([P, NT, EG]),
                                                op0=ALU.is_ge, op1=ALU.mult))
            top(goh, gcode, gtop)
            link(nc.vector.tensor_tensor(emask[:], lg[:, :, EG:].rearrange("p n (g e) -> p n g e", g=EG),
                                         goh[:].unsqueeze(3).to_broadcast([P, NT, EG, EPG]), ALU.mult))
            link(nc.vector.tensor_reduce(esel[:], emask[:].rearrange("p n g e -> p n e g"), AX, ALU.add))
            link(nc.vector.tensor_reduce(emax[:], esel[:], AX, ALU.max))
            nc.vector.tensor_tensor(esh[:], esel[:], wide_n(emax[:], EPG), ALU.subtract).then_inc(esh_ready, 1)
            dve.wait_ge(esh_ready, 1)
            de = desc_e.unsqueeze(1).to_broadcast([P, NT, EPG])
            link(nc.vector.scalar_tensor_tensor(out=ecode[:], in0=esh[:], scalar=0.0, in1=de, op0=ALU.is_ge, op1=ALU.mult))
            top(oh1, ecode, etop)
            link(nc.vector.scalar_tensor_tensor(out=es2[:], in0=oh1[:], scalar=-3.0e38, in1=esh[:], op0=ALU.mult, op1=ALU.add))
            link(nc.vector.tensor_reduce(emax[:], es2[:], AX, ALU.max))
            link(nc.vector.tensor_tensor(ecode[:], es2[:], wide_n(emax[:], EPG), ALU.is_equal))
            link(nc.vector.tensor_tensor(ecode[:], ecode[:], de, ALU.mult))
            top(oh2, ecode, etop)
            link(nc.vector.tensor_tensor(m8[:], oh1[:], oh2[:], ALU.add))
            dve.wait_ge(gexp_ready, 1)
            link(nc.vector.tensor_reduce(gsum[:], gexp[:], AX, ALU.add))
            link(nc.vector.reciprocal(gw[:], gsum[:]))
            dve.wait_ge(eexp_ready, 1)
            link(nc.vector.tensor_tensor(p8[:], eexp[:], m8[:], ALU.mult))
            link(nc.vector.tensor_reduce(den[:], p8[:], AX, ALU.add))
            link(nc.vector.reciprocal(rden[:], den[:]))
            link(nc.vector.tensor_tensor(rden[:], rden[:], gw[:], ALU.mult))
            link(nc.vector.tensor_tensor(p8[:], p8[:], wide_n(rden[:], EPG), ALU.mult))
            g4 = goh[:].unsqueeze(3).to_broadcast([P, NT, EG, EPG])
            link(nc.vector.tensor_tensor(w32[:].rearrange("p n (g e) -> p n g e", g=EG), g4,
                                         p8[:].unsqueeze(2).to_broadcast([P, NT, EG, EPG]), ALU.mult))
            link(nc.vector.tensor_tensor(m32[:], g4, m8[:].unsqueeze(2).to_broadcast([P, NT, EG, EPG]), ALU.mult))
            nc.vector.tensor_copy(m32b[:], m32[:].rearrange("p n g e -> p n (g e)"))
            link(nc.vector.tensor_reduce(msum[:], m32[:].rearrange("p n g e -> p (g e) n"), AX, ALU.add))
            nc.vector.tensor_copy(msumb[:], msum[:])
            nc.vector.tensor_copy(m128[:], msum[:].unsqueeze(2).to_broadcast([P, E, P // E])).then_inc(mask_ready, 1)

            dve.wait_ge(rank_done, 1)
            link(nc.vector.scalar_tensor_tensor(out=pos[:].rearrange("p n e -> p (n e)"), in0=ps[:, 4, 0:NT * E], scalar=1.0,
                                                in1=m32[:].rearrange("p n g e -> p (n g e)"), op0=ALU.add, op1=ALU.mult))
            link(nc.vector.tensor_scalar(pos[:], pos[:], -1.0, None, ALU.add))
            nc.vector.scalar_tensor_tensor(out=key[:], in0=ps[:, 5, 0:1], scalar=float(E), in1=key_col, op0=ALU.mult, op1=ALU.add)
            link(nc.vector.scalar_tensor_tensor(out=keys[:], in0=ps[:, 6, 0:E], scalar=float(E), in1=key_row,
                                                op0=ALU.mult, op1=ALU.add))
            link(nc.vector.tensor_scalar(ahead[:], keys[:], key[:], None, ALU.is_gt))
            link(nc.vector.tensor_reduce(rank[:], ahead[:], AX, ALU.add))
            nc.vector.tensor_scalar(is_first[:], rank[:], PAIRS - 0.5, None, ALU.is_lt)
            nc.vector.tensor_scalar(spot[:], rank[:], -2.0, 2.0 * E - 1, ALU.mult, ALU.add)
            link(nc.vector.tensor_scalar(spot2[:], rank[:], 4.0, 1.0 - 2 * E, ALU.mult, ALU.add))
            link(nc.vector.tensor_tensor(spot2[:], spot2[:], is_first[:], ALU.mult))
            link(nc.vector.tensor_tensor(spot[:], spot[:], spot2[:], ALU.add))
            link(nc.vector.tensor_scalar(unit_of[:], iota_c, spot[:], None, ALU.is_equal))
            nc.vector.tensor_copy(unit_ofb[:], unit_of[:])
            link(nc.vector.tensor_scalar(own_flag[:], ps[:, 5, 0:1], float(CAP), None, ALU.is_gt))
            nc.vector.tensor_scalar(full_ofb[:], unit_of[:], own_flag[:], None, ALU.mult).then_inc(order_ready, 1)
            dve.wait_ge(order_done, 1)
            nc.vector.tensor_scalar(orderf[:].rearrange("p u b -> p (u b)"), ps[:, 7, 0:E], 1.0 / PER, None, ALU.mult)
            link(nc.vector.tensor_scalar(flags[:].unsqueeze(2), ps[:, 7, E:2 * E].rearrange("p (u b) -> p u b", b=2)[:, :, 0:1],
                                         1.0 / PER, None, ALU.mult))
            nc.vector.tensor_copy(order[:], orderf[0:1].rearrange("p u b -> p (u b)"))
            nc.vector.tensor_scalar(shared_r[:], flags[:], float(TILE), float(TILE), ALU.mult, ALU.add)
            nc.vector.tensor_tensor(sharedf[:].unsqueeze(2), orderf[:, :, 0:1], orderf[:, :, 1:2], ALU.subtract)
            link(nc.vector.tensor_scalar(notflag[:], flags[:], -1.0, 1.0, ALU.mult, ALU.add))
            link(nc.vector.tensor_tensor(sharedf[:], sharedf[:], flags[:], ALU.mult))
            link(nc.vector.tensor_tensor(sharedf[:].unsqueeze(2), sharedf[:].unsqueeze(2), orderf[:, :, 1:2], ALU.add))
            nc.vector.tensor_copy(shared_b[:], notflag[0:1])
            nc.vector.tensor_copy(shared_e[:], sharedf[0:1]).then_inc(pairs_ready, 1)
            dve.wait_ge(pairs_ready, 1)

            def select(chain):
                chain(nc.vector.tensor_tensor(self_[:].rearrange("p n (h c) -> p n h c", h=4),
                                              iota_c[:, 0:TILE].unsqueeze(1).unsqueeze(1).to_broadcast([P, NT, 4, TILE]),
                                              pc[:].unsqueeze(3).to_broadcast([P, NT, 4, TILE]), ALU.is_equal))
                nc.vector.tensor_copy(selb[:], self_[:]).then_inc(sel_ready, 1)

            SEL_STEPS = 2

            def select_pair(u, chain):
                first, second = (dve.value_load(order[0:1, bass.ds(u * 2 + ab, 1)], min_val=0, max_val=E - 1)
                                 for ab in range(2))
                shared = dve.value_load(shared_e[0:1, bass.ds(u, 1)], min_val=0, max_val=E - 1)
                nc.vector.tensor_scalar(pc[:, :, 0:1], pos[:, :, bass.ds(shared, 1)], shared_r[:, bass.ds(u, 1)], None, ALU.subtract)
                nc.vector.tensor_copy(pc[:, :, 1:2], pos[:, :, bass.ds(second, 1)])
                nc.vector.tensor_copy(pc[:, :, 2:3], pos[:, :, bass.ds(first, 1)])
                nc.vector.tensor_scalar(pc[:, :, 3:4], pos[:, :, bass.ds(first, 1)], -float(TILE), None, ALU.add)
                for k, e in enumerate((shared, second, first)):
                    last = nc.vector.tensor_copy(wc[:, :, k:k + 1], w32[:, :, bass.ds(e, 1)])
                chain(last)
                select(chain)

            dve.wait_ge(xb2_ready, NT)
            select_pair(0, link)

            link(nc.vector.tensor_tensor(by_unit[:].rearrange("p (u b) -> p u b", b=2),
                                         unit_of[:].rearrange("p (u b) -> p u b", b=2),
                                         flags[:].unsqueeze(2).to_broadcast([P, PAIRS, 2]), ALU.mult))
            nc.vector.tensor_scalar(spot[:], is_first[:], 2.0 * TILE, -float(TILE), ALU.mult, ALU.add)
            link(nc.vector.tensor_reduce(own_flag[:], by_unit[:], AX, ALU.add))
            link(nc.vector.tensor_tensor(first_rank[:], own_flag[:], spot[:], ALU.mult))
            link(nc.vector.tensor_tensor(first_rank[:], first_rank[:], cand_t, ALU.add))
            link(nc.vector.tensor_tensor(active[:], ps[:, 5, 0:1], first_rank[:], ALU.is_gt))
            nc.vector.tensor_copy(activeb[:], active[:]).then_inc(active_ready, 1)
            dve.wait_ge(prefix_done, 1)
            link(nc.vector.tensor_copy(prefix[:], ps[:, 5, 2:3]))
            link(nc.vector.tensor_scalar(unit_oh[:], iota_u, prefix[:], active[:], ALU.is_equal, ALU.mult))
            nc.vector.tensor_copy(unit_ohb[:], unit_oh[:])
            nc.vector.tensor_scalar(unit_rb[:], unit_oh[:], first_rank[:], None, ALU.mult).then_inc(unit_ready, 1)
            dve.wait_ge(table_done, 1)
            nc.vector.tensor_copy(over_e[:], ps[0:1, 4, 0:MAX_OVER])
            nc.vector.tensor_copy(over_r[:], ps[:, 4, MAX_OVER:2 * MAX_OVER])
            link(nc.vector.tensor_reduce(over_nf[:], ps[:, 4, 2 * MAX_OVER:3 * MAX_OVER], AX, ALU.add))
            nc.vector.tensor_copy(over_n[:], over_nf[0:1]).then_inc(table_ready, 1)
            dve.wait_ge(table_ready, 1)

            def take_selection(u):
                dve.wait_ge(seltr_done, u + 1)
                nc.vector.tensor_copy(selt[:].rearrange("p n t -> p (n t)"), ps[:, 6])
                nc.vector.tensor_copy(wsl[0:TILE], ps[0:TILE, 7, 0:1])
                nc.vector.tensor_copy(wsl[TILE:CAP], ps[TILE:CAP, 7, 1:2])
                nc.vector.tensor_copy(wsl[CAP:], ps[CAP:, 7, 2:3]).then_inc(selt_done, 1)

            def hidden(u):
                dve.wait_ge(silu_done, u + 1)
                dve.wait_ge(used, u * USED + 2 * KX)
                dve.wait_ge(selt_done, u + 1)
                nc.vector.scalar_tensor_tensor(out=hh[:], in0=ps[:, 1], scalar=wsl[:], in1=sl[:], op0=ALU.mult,
                                               op1=ALU.mult).then_inc(h_done, 1)

            def take_hidden(u):
                dve.wait_ge(htr_done, u + 1)
                nc.vector.tensor_copy(ht[:].rearrange("p j s -> p (j s)"), ps[:, 0]).then_inc(ht_ready, 1)

            def low_y(u, c):
                dve.wait_ge(yh_done, u * DX + (c + 1))
                nc.vector.tensor_tensor(yl[:, c % 2], ps[:, 2 + c % 2], yh[:, c % 2].bitcast(F32), ALU.subtract
                                        ).then_inc(y_split, 1)

            def add(u, c):
                for n in range(NT):
                    dve.wait_ge(cb_done, u * (DX * NT) + (c * NT + n + 6))
                    hs = h[:, n, c * CB:(c + 1) * CB]
                    nc.vector.tensor_tensor(hs, hs, ps[:, 4 + n], ALU.add).then_inc(add_done, 1)

            def back(u):
                hidden(u)
                take_hidden(u)
                low_y(u, 0)
                for c in range(1, DX):
                    low_y(u, c)
                    add(u, c - 1)
                add(u, DX - 1)

            with dve.Fori(0, PAIRS - 1) as u:
                take_selection(u)
                select_pair(u + 1, chain_in(u, SEL_STEPS, step[0]))
                back(u)
            step[0] += (PAIRS - 1) * SEL_STEPS

            def select_over(i, chain):
                e = dve.value_load(over_e[0:1, bass.ds(i, 1)], min_val=0, max_val=E - 1)
                for k in range(3):
                    nc.vector.tensor_copy(wc[:, :, k:k + 1], w32[:, :, bass.ds(e, 1)])
                chain(nc.vector.tensor_scalar(pc[:, :, 0:1], pos[:, :, bass.ds(e, 1)], over_r[:, bass.ds(i, 1)], None, ALU.subtract))
                for k in range(1, 4):
                    last = nc.vector.tensor_scalar(pc[:, :, k:k + 1], pc[:, :, 0:1], -float(k * TILE), None, ALU.add)
                chain(last)
                select(chain)

            take_selection(PAIRS - 1)
            select_over(0, link)
            back(PAIRS - 1)
            n_over = dve.value_load(over_n[0:1, 0:1], min_val=0, max_val=MAX_OVER - 1)
            OVER_STEPS = 3
            with dve.Fori(0, MAX_OVER - 1) as i:
                with dve.If(i < n_over):
                    u = i + PAIRS
                    take_selection(u)
                    select_over(i + 1, chain_in(i, OVER_STEPS, step[0]))
                    back(u)
            dve.wait_ge(add_done, n_over * (DX * NT) + (PAIRS * DX * NT + NT))
            nc.vector.memset(prefix[:], 0.0).then_inc(moe_done, 1)
            step_end = sem("step_end")
            dve.wait_ge(fg_in, 16)
            end_steps = [0]

            def end_link(ins):
                end_steps[0] += 1
                ins.then_inc(step_end, 1)
                dve.wait_ge(step_end, end_steps[0])

            for m in range(NT):
                norm(m, 3 * NT + m + 1, 2 * NT + 1 + m + 1, end_link)
                nc.vector.scalar_tensor_tensor(out=h[:, m], in0=h[:, m], scalar=rstd[:, m:m + 1], in1=fgbc[:],
                                               op0=ALU.mult, op1=ALU.mult).then_inc(out_ready, 1)


def mixer_stream(w_in, w_branch, w_out):
    import numpy as np
    D, W = w_in.shape[0], w_branch.shape[1]
    blocks = []
    for i in range(W // CB):
        blocks.append((w_in, 4 * W + i * CB))
    for i in range(W // CB):
        blocks += [(w_in, b * W + i * CB) for b in (0, 2, 1)]
    for i in range(W // CB):
        blocks.append((w_in, 3 * W + i * CB))
    for i in range(D // CB):
        for r in range(w_branch.shape[0]):
            blocks += [(w_in, 5 * W + r * D + i * CB), (w_branch[r], i * CB)]
    for i in range(D // CB):
        blocks.append((w_out, i * CB))
    rows = CK * P
    stream = np.empty((sum(w.shape[0] // rows for w, _ in blocks), P, CK * CB), w_in.dtype)
    q = 0
    for w, col in blocks:
        n = w.shape[0] // rows
        stream[q:q + n].reshape(n, P, CK, CB)[:] = w[:, col:col + CB].reshape(n, CK, P, CB).transpose(0, 2, 1, 3)
        q += n
    return stream


def expert_stream(w_gate, w_up, w_down):
    import numpy as np
    E, D, F = w_gate.shape
    KC, DC = D // (EK * P), D // CB
    stream = np.empty((E, 2 * KC + DC, P, EK, CB), w_gate.dtype)
    stream[:, 0:2 * KC:2] = w_gate.reshape(E, KC, EK, P, F).transpose(0, 1, 3, 2, 4)
    stream[:, 1:2 * KC:2] = w_up.reshape(E, KC, EK, P, F).transpose(0, 1, 3, 2, 4)
    stream[:, 2 * KC:] = w_down.reshape(E, EK, P, DC, CB).transpose(0, 3, 2, 1, 4)
    return stream.reshape(E * (2 * KC + DC), P, EK * CB)


def shape_constants(EG, E):
    import numpy as np
    c = np.arange(P)
    per = P // E
    key = np.arange(E - 1, -1, -1.0)
    key[0], key[1] = 2.0 ** 20, -2.0 ** 20
    parts = [np.eye(P), c[:, None] < c[None, :], np.ones((P, P)),
             np.repeat(c[:, None] // per, P, axis=1),
             np.tile(np.arange(E), (P, 1)), np.tile(np.arange(MAX_OVER), (P, 1)),
             np.tile(np.arange(EG, 0, -1), (P, 1)), np.tile(np.arange(E // EG, 0, -1), (P, 1)),
             np.tile(key, (P, 1)), key[c // per][:, None],
             CAP + P * (c[:, None] % per)]
    return np.concatenate(parts, axis=1).astype(np.float32)


def kernel(x, norm1_g, w_in, b_gate, conv_w, ln_v_g, ln_v_b, sgu_w, sgu_b, w_branch, w_out,
           norm2_g, router_g, router_g_b, router_e, router_e_b, w_gate, w_up, w_down, final_g):
    import numpy as _np
    import concourse.bacc as _bacc
    from concourse import mybir as _mybir
    from concourse.bass_utils import run_bass_kernel_spmd as _run

    assert w_in.shape[0] == 1
    D = x.shape[2]
    laid = {
        'x': x,
        'norm1_g': norm1_g,
        'mixer_w': mixer_stream(w_in[0], w_branch[0], w_out[0]),
        'b_gate': b_gate[0].reshape(-1, P).T,
        'conv_w': conv_w[0].reshape(conv_w.shape[1], -1, P).transpose(2, 0, 1),
        'ln_v_g': ln_v_g, 'ln_v_b': ln_v_b, 'sgu_w': sgu_w, 'sgu_b': sgu_b,
        'norm2_g': norm2_g,
        'router_w': _np.concatenate([router_g[0], router_e[0]], axis=1).reshape(D // P, P, -1).transpose(1, 0, 2),
        'router_b': _np.concatenate([router_g_b, router_e_b], axis=1),
        'expert_w': expert_stream(w_gate[0], w_up[0], w_down[0]),
        'final_g': final_g.reshape(1, -1),
        'consts': shape_constants(router_g.shape[2], router_e.shape[2]),
    }
    nc = _bacc.Bacc("TRN2", target_bir_lowering=False, num_devices=1)
    arrays, args = {}, []
    for name, a in laid.items():
        a = _np.ascontiguousarray(a)
        arrays[f"in_{name}_dram"] = a
        args.append(nc.dram_tensor(f"in_{name}_dram", a.shape, _mybir.dt.from_np(a.dtype), kind="ExternalInput").ap())
    args.append(nc.dram_tensor("out_0_dram", x.shape, _mybir.dt.from_np(_np.dtype('float32')), kind="ExternalOutput").ap())
    hybrid_block(nc, *args)
    r = _run(nc, [arrays], core_ids=[0])
    return r.results[0]["out_0_dram"]
```
